# Optimizing a Trainium2 kernel written in Bass

```python
import math
import jax, jax.numpy as jnp
from jax import lax
import numpy as np

D_MODEL = 1024
BATCH = 1
SEQ = 256
DEPTH = 1
DEC_BATCH = 1
DEC_SEQ = 256
PAST_LEN = 128

PLE_DIM = 256
EPS = 1e-6
CONV_K = 4
SSD_HEADS = 16
SSD_HEAD_DIM = 64
SSD_INNER = SSD_HEADS * SSD_HEAD_DIM
SSD_GROUPS = 4
SSD_STATE = 128
SSD_XBC = SSD_INNER + 2 * SSD_GROUPS * SSD_STATE
SSD_CHUNK = 128
GDN_HEADS = 8
GDN_HEAD_DIM = 128
GDN_INNER = GDN_HEADS * GDN_HEAD_DIM
GDN_CHUNK = 64
PEER_HEADS = 8
PEER_KEYS = 128
PEER_EXPERTS = PEER_KEYS * PEER_KEYS
PEER_QDIM = 256
PEER_TOPK = 16
PEER_BLOCK = 128
IN_SIZES = (SSD_INNER, SSD_XBC, 2 * SSD_HEADS, 3 * GDN_INNER, GDN_INNER, 2 * GDN_HEADS, 2 * GDN_HEADS, D_MODEL, D_MODEL)
IN_COLS = sum(IN_SIZES)
IN_SPLITS = tuple(int(s) for s in np.cumsum(IN_SIZES)[:-1])

kernel_name = 'hybrid_bissd_bigdn_peer_encoder'

def rmsnorm(x, g):
    xf = x.astype(jnp.float32)
    y = xf * lax.rsqrt(jnp.mean(xf * xf, axis=-1, keepdims=True) + EPS)
    return (y * g.astype(jnp.float32)).astype(x.dtype)

def centred_depthwise_conv(x, w):
    kk = w.shape[0]
    left = kk // 2
    l = x.shape[1]
    xp = jnp.pad(x, ((0, 0), (left, kk - 1 - left), (0, 0)))
    y = xp[:, 0:l] * w[0]
    for j in range(1, kk):
        y = y + xp[:, j:j + l] * w[j]
    return y

def l2norm(t):
    return t * lax.rsqrt(jnp.sum(t * t, axis=-1, keepdims=True) + EPS)

def ssd_chunked_scan(x, dt, a, bm, cm):
    b, l, h, p = x.shape
    g, n = bm.shape[2], bm.shape[3]
    r = h // g
    q = SSD_CHUNK
    c = l // q
    xd = (x * dt[..., None]).reshape(b, c, q, g, r, p)
    a_cum = jnp.cumsum((dt * a).reshape(b, c, q, g, r), axis=2)
    bc = bm.reshape(b, c, q, g, n)
    cc = cm.reshape(b, c, q, g, n)
    lower = jnp.tril(jnp.ones((q, q), bool))[:, :, None, None]
    seg = a_cum[:, :, :, None] - a_cum[:, :, None, :]
    decay_ls = jnp.exp(jnp.where(lower, seg, -jnp.inf))
    scores = jnp.einsum('bclgn,bcsgn->bclsg', cc, bc)
    mix = scores[..., None] * decay_ls
    y_diag = jnp.einsum('bclsgr,bcsgrp->bclgrp', mix, xd)
    decay_to_end = jnp.exp(a_cum[:, :, -1:] - a_cum)
    chunk_states = jnp.einsum('bcsgn,bcsgrp->bcgrpn', bc, xd * decay_to_end[..., None])
    chunk_decay = jnp.exp(a_cum[:, :, -1])

    def step(state, inp):
        st, dec = inp
        return state * dec[..., None, None] + st, state

    init = jnp.zeros((b, g, r, p, n), x.dtype)
    _, prev = lax.scan(step, init, (jnp.moveaxis(chunk_states, 1, 0), jnp.moveaxis(chunk_decay, 1, 0)))
    prev = jnp.moveaxis(prev, 0, 1)
    y_off = jnp.einsum('bclgn,bcgrpn->bclgrp', cc, prev) * jnp.exp(a_cum)[..., None]
    return (y_diag + y_off).reshape(b, l, h, p)

def ssd_mixer(z, xbc, dt_raw, conv_w, conv_b, a_log, dt_bias, d_skip, norm_w):
    f32 = jnp.float32
    b, l, _ = z.shape
    xbc = jax.nn.silu((centred_depthwise_conv(xbc, conv_w) + conv_b).astype(f32))
    xs, bm, cm = jnp.split(xbc, [SSD_INNER, SSD_INNER + SSD_GROUPS * SSD_STATE], axis=-1)
    xs = xs.reshape(b, l, SSD_HEADS, SSD_HEAD_DIM)
    bm = bm.reshape(b, l, SSD_GROUPS, SSD_STATE)
    cm = cm.reshape(b, l, SSD_GROUPS, SSD_STATE)
    dt_f, dt_b = jnp.split(dt_raw.astype(f32), 2, axis=-1)
    dt_bias = dt_bias.astype(f32)
    dt_f = jax.nn.softplus(dt_f + dt_bias[0])
    dt_b = jax.nn.softplus(dt_b + dt_bias[1])
    a = -jnp.exp(a_log.astype(f32))
    fl = lambda t: jnp.flip(t, axis=1)
    y = ssd_chunked_scan(xs, dt_f, a[0], bm, cm) + fl(ssd_chunked_scan(fl(xs), fl(dt_b), a[1], fl(bm), fl(cm)))
    y = y + xs * d_skip.astype(f32)[:, None]
    y = y.reshape(b, l, SSD_INNER) * jax.nn.silu(z.astype(f32))
    yg = y.reshape(b, l, SSD_GROUPS, SSD_INNER // SSD_GROUPS)
    yg = yg * lax.rsqrt(jnp.mean(yg * yg, axis=-1, keepdims=True) + EPS)
    return (yg.reshape(b, l, SSD_INNER) * norm_w.astype(f32)).astype(z.dtype)

def gated_delta_chunked(q, k, v, g, beta):
    b, h, l, dk = q.shape
    dv = v.shape[-1]
    c = GDN_CHUNK
    n = l // c
    q = q * dk ** -0.5
    q, k, v = (t.reshape(b, h, n, c, t.shape[-1]) for t in (q, k, v))
    g, beta = (t.reshape(b, h, n, c) for t in (g, beta))
    kb = k * beta[..., None]
    vb = v * beta[..., None]
    dec = jnp.cumsum(g, axis=-1)
    incl = jnp.tril(jnp.ones((c, c), bool))
    strict = jnp.tril(jnp.ones((c, c), bool), -1)
    gam = jnp.exp(jnp.where(incl, dec[..., :, None] - dec[..., None, :], -jnp.inf))
    a_low = jnp.where(strict, jnp.einsum('bhnid,bhnjd->bhnij', kb, k) * gam, 0.0)
    eye = jnp.eye(c, dtype=q.dtype)
    t_inv = lax.linalg.triangular_solve(a_low + eye, jnp.broadcast_to(eye, a_low.shape),
                                        left_side=True, lower=True, unit_diagonal=True)
    u = t_inv @ vb
    w = t_inv @ (kb * jnp.exp(dec)[..., None])
    qk = jnp.einsum('bhnid,bhnjd->bhnij', q, k) * gam
    q_dec = q * jnp.exp(dec)[..., None]
    k_dec = k * jnp.exp(dec[..., -1:] - dec)[..., None]
    last = jnp.exp(dec[..., -1])

    def step(s, inp):
        u_c, w_c, qk_c, qd_c, kd_c, last_c = inp
        v_new = u_c - jnp.einsum('bhck,bhkv->bhcv', w_c, s)
        o = jnp.einsum('bhck,bhkv->bhcv', qd_c, s) + jnp.einsum('bhcs,bhsv->bhcv', qk_c, v_new)
        s = s * last_c[..., None, None] + jnp.einsum('bhck,bhcv->bhkv', kd_c, v_new)
        return s, o

    xs = tuple(jnp.moveaxis(t, 2, 0) for t in (u, w, qk, q_dec, k_dec, last))
    _, o = lax.scan(step, jnp.zeros((b, h, dk, dv), q.dtype), xs)
    return jnp.moveaxis(o, 0, 2).reshape(b, h, l, dv)

def gdn_mixer(qkv, z, a_raw, beta_raw, conv_w, a_log, dt_bias, norm_w):
    f32 = jnp.float32
    b, l, _ = z.shape
    qkv = jax.nn.silu(centred_depthwise_conv(qkv, conv_w).astype(f32))
    q, k, v = jnp.split(qkv, 3, axis=-1)
    heads = lambda t: t.reshape(b, l, GDN_HEADS, GDN_HEAD_DIM).transpose(0, 2, 1, 3)
    q, k, v = l2norm(heads(q)), l2norm(heads(k)), heads(v)
    a_f, a_b = jnp.split(a_raw.astype(f32), 2, axis=-1)
    beta_f, beta_b = jnp.split(jax.nn.sigmoid(beta_raw.astype(f32)), 2, axis=-1)
    a_coef = jnp.exp(a_log.astype(f32))
    dt_bias = dt_bias.astype(f32)
    g_f = -a_coef[0] * jax.nn.softplus(a_f + dt_bias[0])
    g_b = -a_coef[1] * jax.nn.softplus(a_b + dt_bias[1])
    tr = lambda t: t.transpose(0, 2, 1)
    fl = lambda t: jnp.flip(t, axis=2)
    o = gated_delta_chunked(q, k, v, tr(g_f), tr(beta_f)) + fl(
        gated_delta_chunked(fl(q), fl(k), fl(v), fl(tr(g_b)), fl(tr(beta_b))))
    o = o.transpose(0, 2, 1, 3)
    o = o * lax.rsqrt(jnp.mean(o * o, axis=-1, keepdims=True) + EPS) * norm_w.astype(f32)
    o = o.reshape(b, l, GDN_INNER) * jax.nn.silu(z.astype(f32))
    return o.astype(z.dtype)

def peer_ffn(x, w_query, sub_keys, expert_u, expert_v):
    f32 = jnp.float32
    b, l, d = x.shape
    t = x.reshape(b * l, d)
    nt = t.shape[0]
    qry = (t @ w_query).reshape(nt, PEER_HEADS, 2, PEER_QDIM // 2)
    s = jnp.einsum('thzd,hzkd->thzk', qry.astype(f32), sub_keys.astype(f32))
    top_s, top_i = lax.top_k(s, PEER_TOPK)
    kk = PEER_TOPK * PEER_TOPK
    cand_s = (top_s[:, :, 0, :, None] + top_s[:, :, 1, None, :]).reshape(nt, PEER_HEADS, kk)
    cand_i = (top_i[:, :, 0, :, None] * PEER_KEYS + top_i[:, :, 1, None, :]).reshape(nt, PEER_HEADS, kk)
    best_s, best_pos = lax.top_k(cand_s, PEER_TOPK)
    idx = jnp.take_along_axis(cand_i, best_pos, axis=-1)
    gate = jax.nn.softmax(best_s, axis=-1)
    nb = nt // PEER_BLOCK

    def block(args):
        tb, ib, gb = args
        act = jax.nn.gelu(jnp.einsum('td,thkd->thk', tb, expert_u[ib]).astype(f32), approximate=False)
        wts = (act * gb).astype(tb.dtype)
        return jnp.einsum('thk,thkd->td', wts, expert_v[ib])

    out = lax.map(block, (t.reshape(nb, PEER_BLOCK, d),
                          idx.reshape(nb, PEER_BLOCK, PEER_HEADS, PEER_TOPK),
                          gate.reshape(nb, PEER_BLOCK, PEER_HEADS, PEER_TOPK)))
    return out.reshape(b, l, d).astype(x.dtype)

def encoder_layer(h, ple, W, i):
    f32 = jnp.float32
    n1 = rmsnorm(h, W['norm_mix'][i])
    proj = n1 @ W['w_in'][i]
    ssd_z, ssd_xbc, ssd_dt, gdn_qkv, gdn_z, gdn_a, gdn_beta, gate_a, gate_b = jnp.split(proj, IN_SPLITS, axis=-1)
    y_a = ssd_mixer(ssd_z, ssd_xbc, ssd_dt, W['ssd_conv_w'][i], W['ssd_conv_b'][i], W['ssd_a_log'][i],
                    W['ssd_dt_bias'][i], W['ssd_d'][i], W['ssd_norm'][i]) @ W['w_ssd_out'][i]
    y_b = gdn_mixer(gdn_qkv, gdn_z, gdn_a, gdn_beta, W['gdn_conv_w'][i], W['gdn_a_log'][i],
                    W['gdn_dt_bias'][i], W['gdn_norm'][i]) @ W['w_gdn_out'][i]
    merged = (jax.nn.sigmoid(gate_a.astype(f32)) * y_a.astype(f32)
              + jax.nn.sigmoid(gate_b.astype(f32)) * y_b.astype(f32))
    h = h + (merged.astype(h.dtype) @ W['w_out'][i]).astype(h.dtype)
    h = h + peer_ffn(rmsnorm(h, W['norm_ffn'][i]), W['peer_query'][i], W['peer_keys'][i],
                     W['expert_u'][i], W['expert_v'][i]).astype(h.dtype)
    ple_gate = jax.nn.sigmoid((rmsnorm(h, W['norm_ple'][i]) @ W['w_ple_gate'][i]).astype(f32))
    h = h + (ple_gate * (ple @ W['w_ple_proj'][i]).astype(f32)).astype(h.dtype)
    return h

def encoder_trunk(x, ple, W, norm_final):
    h = x
    for i in range(DEPTH):
        h = encoder_layer(h, ple[i], W, i)
    return rmsnorm(h, norm_final)

def setup_inputs(seed: int = 0) -> dict:
    key = jax.random.key(seed)
    ks = iter(jax.random.split(key, 40))
    f32 = jnp.float32
    L = DEPTH

    def nrm(shape, scale):
        return jax.random.normal(next(ks), shape, f32) * scale

    def gain(shape):
        return 1.0 + nrm(shape, 0.02)

    def log_uniform(shape, lo, hi):
        return jnp.log(jax.random.uniform(next(ks), shape, f32, lo, hi))

    def dt_bias_init(shape):
        dt = jnp.exp(jax.random.uniform(next(ks), shape, f32, math.log(1e-3), math.log(1e-1)))
        return dt + jnp.log(-jnp.expm1(-dt))

    return {
        'x_prompt': nrm((BATCH, SEQ, D_MODEL), 1.0),
        'x_sample': nrm((DEC_BATCH, DEC_SEQ, D_MODEL), 1.0),
        'p_prompt': nrm((DEPTH, BATCH, SEQ, PLE_DIM), 1.0),
        'p_sample': nrm((DEPTH, DEC_BATCH, DEC_SEQ, PLE_DIM), 1.0),
        'norm_mix': gain((L, D_MODEL)),
        'w_in': nrm((L, D_MODEL, IN_COLS), D_MODEL ** -0.5),
        'ssd_conv_w': nrm((L, CONV_K, SSD_XBC), CONV_K ** -0.5),
        'ssd_conv_b': nrm((L, SSD_XBC), 0.02),
        'ssd_a_log': log_uniform((L, 2, SSD_HEADS), 1.0, 16.0),
        'ssd_dt_bias': dt_bias_init((L, 2, SSD_HEADS)),
        'ssd_d': 1.0 + nrm((L, SSD_HEADS), 0.1),
        'ssd_norm': gain((L, SSD_INNER)),
        'w_ssd_out': nrm((L, SSD_INNER, D_MODEL), SSD_INNER ** -0.5),
        'gdn_conv_w': nrm((L, CONV_K, 3 * GDN_INNER), CONV_K ** -0.5),
        'gdn_a_log': log_uniform((L, 2, GDN_HEADS), 1.0, 16.0),
        'gdn_dt_bias': dt_bias_init((L, 2, GDN_HEADS)),
        'gdn_norm': gain((L, GDN_HEAD_DIM)),
        'w_gdn_out': nrm((L, GDN_INNER, D_MODEL), GDN_INNER ** -0.5),
        'w_out': nrm((L, D_MODEL, D_MODEL), D_MODEL ** -0.5),
        'norm_ffn': gain((L, D_MODEL)),
        'peer_query': nrm((L, D_MODEL, PEER_HEADS * PEER_QDIM), D_MODEL ** -0.5),
        'peer_keys': nrm((L, PEER_HEADS, 2, PEER_KEYS, PEER_QDIM // 2), (PEER_QDIM // 2) ** -0.5),
        'expert_u': nrm((L, PEER_EXPERTS, D_MODEL), D_MODEL ** -0.5),
        'expert_v': nrm((L, PEER_EXPERTS, D_MODEL), PEER_HEADS ** -0.5),
        'norm_ple': gain((L, D_MODEL)),
        'w_ple_gate': nrm((L, D_MODEL, D_MODEL), D_MODEL ** -0.5),
        'w_ple_proj': nrm((L, PLE_DIM, D_MODEL), PLE_DIM ** -0.5),
        'norm_final': gain((D_MODEL,)),
    }

def reference(x_prompt, x_sample, p_prompt, p_sample, norm_mix, w_in, ssd_conv_w, ssd_conv_b, ssd_a_log,
              ssd_dt_bias, ssd_d, ssd_norm, w_ssd_out, gdn_conv_w, gdn_a_log, gdn_dt_bias, gdn_norm, w_gdn_out,
              w_out, norm_ffn, peer_query, peer_keys, expert_u, expert_v, norm_ple, w_ple_gate, w_ple_proj,
              norm_final):
    W = dict(norm_mix=norm_mix, w_in=w_in, ssd_conv_w=ssd_conv_w, ssd_conv_b=ssd_conv_b, ssd_a_log=ssd_a_log,
             ssd_dt_bias=ssd_dt_bias, ssd_d=ssd_d, ssd_norm=ssd_norm, w_ssd_out=w_ssd_out, gdn_conv_w=gdn_conv_w,
             gdn_a_log=gdn_a_log, gdn_dt_bias=gdn_dt_bias, gdn_norm=gdn_norm, w_gdn_out=w_gdn_out, w_out=w_out,
             norm_ffn=norm_ffn, peer_query=peer_query, peer_keys=peer_keys, expert_u=expert_u, expert_v=expert_v,
             norm_ple=norm_ple, w_ple_gate=w_ple_gate, w_ple_proj=w_ple_proj)
    y_prompt = encoder_trunk(x_prompt, p_prompt, W, norm_final)
    y_sample = encoder_trunk(x_sample, p_sample, W, norm_final)
    return (y_prompt, y_sample)


_drawn_inputs = setup_inputs


def setup_inputs(seed=0):
    import zlib

    import numpy as np

    out = dict(_drawn_inputs(seed))
    spreads = {}
    factors = {'ssd_norm': 33.62,
     'gdn_norm': 54.352,
     'norm_ple': 200.0,
     'norm_final': 29.929,
     'norm_ffn': 17.356}
    for name, (base, spread) in spreads.items():
        noise = np.random.default_rng([zlib.crc32(name.encode()), seed]).standard_normal(out[name].shape)
        drawn = base * np.exp(spread * noise) if base else spread * noise
        out[name] = __import__('jax').numpy.asarray(drawn.astype(out[name].dtype))
    for name, factor in factors.items():
        out[name] = (out[name] * factor).astype(out[name].dtype)
    return out
```

```python
from contextlib import ExitStack

import numpy as np

import concourse.bass as bass
from concourse import mybir
from concourse.alu_op_type import AluOpType as ALU

ACT = mybir.ActivationFunctionType
AX = mybir.AxisListType
F32 = mybir.dt.float32
F32R = mybir.dt.float32r
U32 = mybir.dt.uint32

P = 128
SEQS = 2
L = 256
T = SEQS * L
TT = T // P
TS = L // P
D = 1024
KT = D // P
PLE = 256
EPS = 1e-6
SSD_H, SSD_P, SSD_G, SSD_N = 16, 64, 4, 128
SSD_R = SSD_H // SSD_G
GDN_H, GDN_D = 8, 128
PEER_H, PEER_K, PEER_Q, TOPK = 8, 128, 256, 16
NHZ = 2 * PEER_H
HK = PEER_H * TOPK
CW = 512
N_CONV = (SSD_H * SSD_P + 2 * SSD_G * SSD_N + 3 * GDN_H * GDN_D) // P
NEG = -3.0e38

SQUARES = ["eye", "ones", "le", "ge", "lt", "gt"] + [f"lvl{b}" for b in (1, 2, 4, 8, 16, 32, 64)] + ["iota"]
LEVELS = (2, 4, 8, 16, 32, 64)

COL_CONV = 0
COL_MIX = COL_CONV + 5 * N_CONV
COL_FFN = COL_MIX + KT
COL_PLE = COL_FFN + KT
COL_SSDN = COL_PLE + KT
COL_GDNN = COL_SSDN + KT
COLS = COL_GDNN + 1

ROW_BIAS = 0
ROW_ALOG = 48
ROW_D = 96
ROWS = 112


def squares():
    p, c = np.arange(P)[:, None], np.arange(P)[None, :]
    m = {"eye": p == c, "ones": p == p + 0 * c, "le": p <= c, "ge": p >= c, "lt": p < c, "gt": p > c, "iota": c + 0 * p}
    for b in (1, 2, 4, 8, 16, 32, 64):
        m[f"lvl{b}"] = (p // (2 * b) == c // (2 * b)) & (p // b != c // b)
    return np.concatenate([np.broadcast_to(m[k], (P, P)).astype(np.float32) for k in SQUARES], axis=1)


class Steps:

    def __init__(self, eng, sem, passed=None):
        self.eng, self.sem, self.base, self.k, self.i, self.per, self.passed = eng, sem, 0, 0, None, 0, passed

    def loop(self, i, per):
        self.i, self.per, self.base, self.k = i, per, self.base + self.k, 0

    def end(self, trips):
        assert self.k == self.per, (self.k, self.per)
        self.base, self.k, self.i = self.base + trips * self.per, 0, None

    def value(self):
        return self.base + self.k if self.i is None else self.i * self.per + (self.base + self.k)

    def done(self, ins):
        self.k += 1
        ins.then_inc(self.sem, 1)
        self.eng.wait_ge(self.sem, self.value())
        if self.passed is not None:
            self.eng.sem_inc(self.passed, 1)


def hold(eng, m, sem, value):
    eng.wait_ge(sem, value)
    eng.sem_inc(m.held[eng.engine], 1)


class Region:

    def __init__(self, nc, start, end):
        self.nc, self.at, self.end = nc, start, end

    def take(self, name, shape, dt=F32):
        size = 4 * int(np.prod(shape[1:]))
        size += -size % 32
        assert self.at + size <= self.end, (name, self.at + size - self.end)
        t = self.nc.alloc_sbuf_tensor_at(f"{name}_sb", shape, dt, offset=self.at)
        self.at += size
        return t


def bits32(x):
    return x.bitcast(F32)


class M:
    pass


KB = 1024
AT_XT, AT_OG, AT_CH, AT_WORK, AT_END = 57.25, 73.25, 89.25, 169.25, 222.5
AT_SCORES = 57.25
KB_GATES = 64
DOWN_J = 4


def build(nc, ins, outs, last_stage=99):
    m = M()
    m.ins, m.outs, m.sems = ins, outs, []
    base = nc.sbuf_base + -nc.sbuf_base % 64

    def sem(name):
        m.sems.append(nc.alloc_semaphore(name=name))
        return m.sems[-1]

    def region(start, end):
        return Region(nc, base + int(start * KB), base + int(end * KB))

    m.sem, m.region = sem, region
    m.held = {e.engine: nc.alloc_semaphore(name=n) for e, n in ((nc.scalar, "act_passed_a_wait"), (nc.gpsimd, "pool_passed_a_wait"))}
    r = region(0, AT_XT)
    m.sq = r.take("squares", [P, len(SQUARES), P])
    m.colp = r.take("column_params", [P, COLS])
    m.rowp = r.take("row_params", [P, ROWS])
    m.h = r.take("h", [P, TT, D])
    m.nh = r.take("n_high", [P, KT, T], F32R)
    m.nl = r.take("n_low", [P, KT, T], F32R)
    m.stat = r.take("stat", [P, 3, TT])
    m.eps = r.take("eps", [P, 1])
    m.ps = nc.alloc_psum_tensor("ps", [P, 8, CW], F32)
    for n, stage in enumerate([input_stage, mixer_stages, expert_stages, output_stage]):
        if n <= last_stage:
            stage(nc, m, last_stage)
            end_stage(nc, m)


def products(pe, out, stationary, moving):
    n = len(stationary)
    for k, ((ah, al), (bh, bl)) in enumerate(zip(stationary, moving)):
        pe.matmul(out, ah, bh, start=k == 0, stop=False)
        pe.matmul(out, ah, bl, start=False, stop=False)
        last = pe.matmul(out, al, bh, start=False, stop=k == n - 1)
    return last


def sq(m, name):
    return m.sq[:, SQUARES.index(name), :]


def sq_pair(m, name, mid):
    n = SQUARES.index(name)
    return m.sq[:, n:n + 2, :].unsqueeze(2).broadcast_to([P, 2, mid, P])


def end_stage(nc, m):
    nc.clear_and_free_semaphores(m.sems)
    m.sems = []
    nc.all_engine_barrier()


class NormT:

    def __init__(self, nc, m, region, tag, col):
        self.nc, self.m, self.col = nc, m, col
        self.xs = region.take(f"{tag}_scaled", [P, TT, D])
        (self.sq_done, self.ms_done, self.root_done, self.vec, self.scaled, self.turned, self.high_done, self.out_done) = (
            m.sem(f"{tag}_{x}") for x in ("squares_done", "mean_done", "root_done", "vector_steps", "scaled_done", "turned",
                                          "high_done", "low_done"))

    def act(self, act, ready=lambda tt: None):
        m = self.m
        for tt in range(TT):
            ready(tt)
            act.activation(self.xs[:, tt, :], m.h[:, tt, :], ACT.Square,
                           accum_out=m.stat[:, 0, tt:tt + 1]).then_inc(self.sq_done, 1)
        act.wait_ge(self.ms_done, 1)
        act.activation(m.stat[:, 2, :], m.stat[:, 1, :], ACT.Sqrt).then_inc(self.root_done, 1)
        for kt in range(KT):
            act.wait_ge(self.turned, kt + 1)
            act.activation(m.nh[:, kt, :], m.ps[:, kt, :], ACT.Copy,
                           scale=m.colp[:, self.col + kt:self.col + kt + 1]).then_inc(self.high_done, 1)

    def dve(self, dve):
        m, st = self.m, Steps(dve, self.vec)
        dve.wait_ge(self.sq_done, TT)
        dve.tensor_scalar(m.stat[:, 1, :], m.stat[:, 0, :], 1.0 / D, EPS, ALU.mult, ALU.add).then_inc(self.ms_done, 1)
        dve.wait_ge(self.root_done, 1)
        st.done(dve.reciprocal(m.stat[:, 0, :], m.stat[:, 2, :]))
        for tt in range(TT):
            dve.tensor_scalar(self.xs[:, tt, :], m.h[:, tt, :], m.stat[:, 0, tt:tt + 1], None,
                              ALU.mult).then_inc(self.scaled, 1)
        for kt in range(KT):
            dve.wait_ge(self.high_done, kt + 1)
            dve.scalar_tensor_tensor(m.nl[:, kt, :], m.ps[:, kt, :], m.colp[:, self.col + kt:self.col + kt + 1],
                                     bits32(m.nh[:, kt, :]), ALU.mult, ALU.subtract).then_inc(self.out_done, 1)

    def pe(self, pe):
        m = self.m
        pe.wait_ge(self.scaled, TT)
        for kt in range(KT):
            for tt in range(TT):
                last = pe.transpose(m.ps[:, kt, tt * P:(tt + 1) * P], self.xs[:, tt, kt * P:(kt + 1) * P], sq(m, "eye"))
            last.then_inc(self.turned, 1)


def input_stage(nc, m, last_stage):
    with ExitStack() as ctx:
        norm = NormT(nc, m, m.region(AT_XT, AT_OG), "mix_norm", COL_MIX)
        const_in, x_in = m.sem("constants_loaded"), m.sem("tokens_loaded")
        block = ctx.enter_context(nc.Block())

        @block.gpsimd
        def _(pool):
            pool.memset(m.eps[:, :], EPS)

        @block.sync
        def _(sp):
            for tt in range(TT):
                x = m.ins["x_prompt"] if tt < TS else m.ins["x_sample"]
                sp.dma_start(m.h[:, tt, :], x[0, (tt % TS) * P:(tt % TS + 1) * P, :]).then_inc(x_in, 16)
            sp.dma_start(m.sq[:, :, :], m.ins["squares"].rearrange("p (n c) -> p n c", c=P)).then_inc(const_in, 16)
            sp.dma_start(m.colp[:, :], m.ins["column_params"]).then_inc(const_in, 16)
            sp.dma_start(m.rowp[:, :], m.ins["row_params"].broadcast_to([P, ROWS])).then_inc(const_in, 16)

        @block.scalar
        def _(act):
            def ready(tt):
                if tt == 0:
                    act.wait_ge(x_in, 16 * TT)
                    act.wait_ge(const_in, 48)
            norm.act(act, ready)

        @block.vector
        def _(dve):
            dve.wait_ge(x_in, 16 * TT)
            norm.dve(dve)

        @block.tensor
        def _(pe):
            pe.wait_ge(const_in, 48)
            norm.pe(pe)


def mixer_stages(nc, m, last_stage):
    m.xt = m.region(AT_XT, AT_OG).take("ssd_tokens", [P, TT, D])
    m.og = m.region(AT_OG, AT_CH).take("gdn_tokens", [P, TT, D])
    m.ch = m.region(AT_CH, AT_WORK).take("channels", [P, N_CONV, T])
    r = m.region(AT_END - 4.25, AT_END)
    m.small = r.take("small", [P, TT, 64])
    m.decay = r.take("decay", [P, TT, 48])
    m.edk = r.take("gdn_decays", [P, 4, TT, 16])
    m.ned = r.take("gdn_neg_decay", [P, 2, TT, 16])
    for n, stage in enumerate((project_stage, turn_stage, ssd_stage, gdn_stage, merge_stage)):
        if last_stage > 1 + n * 0.1:
            stage(nc, m)
            end_stage(nc, m)


def log1p_coeffs():
    return [1.0 / (2 * n + 1) for n in range(0, 10)]


def project_stage(nc, m):
    CC = 2 * P
    CHUNKS = 4
    TILES = CHUNKS * 2
    TRIPS = N_CONV // TILES
    raw_r, split_r = m.region(AT_XT, AT_CH), m.region(AT_WORK, AT_END - 4.25)
    w = raw_r.take("w_slots", [P, 2, KT, CC])
    tmp = raw_r.take("small_tmp", [P, 5, TT, 48])
    ws = raw_r.take("w_small", [P, KT, 64])
    wsh, wsl = raw_r.take("w_small_high", [P, KT, 64], F32R), raw_r.take("w_small_low", [P, KT, 64], F32R)
    tab = raw_r.take("a_coefficients", [P, 48])
    wh, wl = split_r.take("w_high", [P, 2, KT, CC], F32R), split_r.take("w_low", [P, 2, KT, CC], F32R)
    w_in = [m.sem(f"w_slot{j}_loaded") for j in range(2)]
    ws_in, small_high, small_low = m.sem("w_small_loaded"), m.sem("w_small_high"), m.sem("w_small_low")
    high, low = m.sem("w_high_done"), m.sem("w_low_done")
    prod, taps0, conv = m.sem("channels_product"), m.sem("centre_tap"), m.sem("other_taps")
    act_s, dve_s, act_small, dve_small = (m.sem(x) for x in ("conv_act_steps", "conv_dve_steps", "small_act", "small_dve"))
    small_prod, small_out, gate_out = m.sem("small_product"), m.sem("small_copied"), m.sem("gdn_decay_products")
    par = m.colp[:, COL_CONV:COL_MIX].rearrange("p (c k) -> p c k", k=5)

    def tap(c, k):
        return par[:, bass.ds(c, 1), k:k + 1].rearrange("p a b -> p (a b)")

    with nc.Block() as block:

        @block.sync
        def _(sp):
            sp.dma_start(ws[:, :, :], m.ins["w_small"].rearrange("p (k n) -> p k n", n=64)).then_inc(ws_in, 16)

            def load(i, c):
                src = m.ins["w_conv"][bass.ds(i * CHUNKS + c, 1)].rearrange("a p (k n) -> p (a k) n", n=CC)
                sp.dma_start(w[:, c % 2, :, :], src).then_inc(w_in[c % 2], 16)

            for c in range(2):
                load(0, c)
            for c in range(2, CHUNKS):
                sp.wait_ge(low, c - 1)
                load(0, c)
            with sp.Fori(1, TRIPS) as i:
                for c in range(CHUNKS):
                    sp.wait_ge(low, i * CHUNKS + (c - 1))
                    load(i, c)

        @block.gpsimd
        def _(pool):
            pool.wait_ge(small_high, 1)
            pool.tensor_tensor(wsl[:, :, :], ws[:, :, :], bits32(wsh[:, :, :]), ALU.subtract).then_inc(small_low, 1)
            with pool.Fori(0, TRIPS) as i:
                for c in range(CHUNKS):
                    pool.wait_ge(high, i * CHUNKS + (c + 1))
                    pool.tensor_tensor(wl[:, c % 2, :, :], w[:, c % 2, :, :], bits32(wh[:, c % 2, :, :]),
                                       ALU.subtract).then_inc(low, 1)

        @block.tensor
        def _(pe):
            pe.wait_ge(small_low, 1)
            for tt in range(TT):
                t = slice(tt * P, (tt + 1) * P)
                last = products(pe, m.ps[:, 0, tt * 64:(tt + 1) * 64], [(m.nh[:, k, t], m.nl[:, k, t]) for k in range(KT)],
                                [(wsh[:, k, :], wsl[:, k, :]) for k in range(KT)])
            last.then_inc(small_prod, 1)
            pe.wait_ge(dve_small, 1)
            g = m.decay[:, :, 32:48]
            for n, mask in enumerate(("le", "ge", "gt", "lt")):
                last = pe.matmul(m.ps[:, 1, n * 64:(n + 1) * 64], sq(m, mask), g, start=True, stop=True)
            last.then_inc(gate_out, 1)
            pe.wait_ge(act_small, 1)
            with pe.Fori(0, TRIPS) as i:
                for t in range(TILES):
                    j = (t // 2) % 2
                    if t % 2 == 0:
                        pe.wait_ge(low, i * CHUNKS + (t // 2 + 1))
                    pe.wait_ge(conv, i * TILES + (t + 1))
                    f = slice((t % 2) * P, (t % 2 + 1) * P)
                    products(pe, m.ps[:, t, :], [(wh[:, j, k, f], wl[:, j, k, f]) for k in range(KT)],
                             [(m.nh[:, k, :], m.nl[:, k, :]) for k in range(KT)]).then_inc(prod, 1)

        @block.scalar
        def _(act):
            st = Steps(act, act_s)
            act.wait_ge(ws_in, 16)
            act.activation(wsh[:, :, :], ws[:, :, :], ACT.Copy).then_inc(small_high, 1)
            for c in range(2):
                act.wait_ge(w_in[c], 16)
                act.activation(wh[:, c, :, :], w[:, c, :, :], ACT.Copy).then_inc(high, 1)
            act.wait_ge(small_prod, 1)
            act.activation(m.small[:, :, :], m.ps[:, 0, 0:TT * 64].rearrange("p (t n) -> p t n", n=64),
                           ACT.Copy).then_inc(small_out, 1)
            st.done(act.activation(tab[:, :], m.rowp[:, ROW_ALOG:ROW_ALOG + 48], ACT.Exp))
            act.wait_ge(dve_s, 3)
            st.done(act.activation(tmp[:, 2, :, :], tmp[:, 1, :, :], ACT.Exp))
            act.wait_ge(small_out, 1)
            act.wait_ge(gate_out, 1)
            act.activation(m.edk[:, :, :, :], m.ps[:, 1, 0:256].rearrange("p (a t n) -> p a t n", a=4, n=16),
                           ACT.Exp).then_inc(act_small, 1)
            st.done(act.activation(m.small[:, :, 48:64], m.small[:, :, 48:64], ACT.Sigmoid))

            def body(i, last):
                st.loop(0 if last else i, TILES)

                def silu(t):
                    hold(act, m, conv, i * TILES + (TILES + t + 1))
                    ct = m.ch[:, bass.ds(i * TILES + t, 1), :]
                    st.done(act.activation(ct, ct, ACT.Silu))

                for t in range(TILES):
                    hold(act, m, prod, i * TILES + (t + 1))
                    c = i * TILES + t
                    act.activation(m.ch[:, bass.ds(c, 1), :], m.ps[:, t:t + 1, :], ACT.Identity,
                                   bias=tap(c, 4), scale=tap(c, 2)).then_inc(taps0, 1)
                    if t % 2 == 1 and not (last and t >= TILES - 4):
                        j = (t // 2) % 2
                        act.wait_ge(w_in[j], i * 32 + (16 * ((t // 2 + 2) // 2) + 16))
                        act.activation(wh[:, j, :, :], w[:, j, :, :], ACT.Copy).then_inc(high, 1)
                    if t:
                        silu(t - 1)
                silu(TILES - 1)

            with act.Fori(0, TRIPS - 1) as i:
                body(i, False)
            st.end(TRIPS - 1)
            body(TRIPS - 1, True)

        @block.vector
        def _(dve):
            st = Steps(dve, dve_s)
            dve.sem_inc(conv, TILES)
            bias = m.rowp[:, ROW_BIAS:ROW_BIAS + 48].unsqueeze(1).broadcast_to([P, TT, 48])
            z, nz, e, s, q = (tmp[:, n, :, :] for n in range(5))
            dve.wait_ge(small_out, 1)
            st.done(dve.tensor_tensor(z, m.small[:, :, 0:48], bias, ALU.add))
            st.done(dve.tensor_scalar(nz, z, -1.0, None, ALU.mult))
            st.done(dve.tensor_tensor(nz, nz, z, ALU.min))
            dve.wait_ge(act_s, 2)
            st.done(dve.tensor_scalar(nz, e, 2.0, None, ALU.add))
            st.done(dve.reciprocal(nz, nz))
            st.done(dve.tensor_tensor(s, e, nz, ALU.mult))
            st.done(dve.tensor_tensor(e, s, s, ALU.mult))
            co = log1p_coeffs()
            st.done(dve.tensor_scalar(q, e, co[-1], None, ALU.mult))
            for c in co[-2:0:-1]:
                st.done(dve.scalar_tensor_tensor(q, q, c, e, ALU.add, ALU.mult))
            st.done(dve.scalar_tensor_tensor(q, q, co[0], s, ALU.add, ALU.mult))
            st.done(dve.tensor_scalar(z, z, 0.0, None, ALU.max))
            st.done(dve.scalar_tensor_tensor(m.small[:, :, 0:48], q, 2.0, z, ALU.mult, ALU.add))
            st.done(dve.tensor_scalar(tab[:, :], tab[:, :], -1.0, None, ALU.mult))
            dve.tensor_tensor(m.decay[:, :, :], m.small[:, :, 0:48], tab[:, :].unsqueeze(1).broadcast_to([P, TT, 48]),
                              ALU.mult).then_inc(dve_small, 1)
            dve.wait_ge(act_small, 1)
            st.done(dve.tensor_scalar(m.ned[:, :, :, :], m.edk[:, 0:2, :, :], -1.0, None, ALU.mult))
            with dve.Fori(0, TRIPS) as i:
                st.loop(i, 2 * TILES)
                for t in range(TILES):
                    c = i * TILES + t
                    y = m.ch[:, bass.ds(c, 1), :].rearrange("p a (s l) -> p (a s) l", l=L)
                    x = m.ps[:, t, :].rearrange("p (s l) -> p s l", l=L)
                    dve.wait_ge(taps0, i * TILES + (t + 1))
                    for n, (k, lo, hi) in enumerate(((0, 2, 0), (1, 1, 0), (3, 0, 1))):
                        yy = y[:, :, lo:L - hi]
                        xx = x[:, :, 0:L - lo] if lo else x[:, :, hi:L]
                        op = dve.scalar_tensor_tensor(yy, xx, tap(c, k), yy, ALU.mult, ALU.add)
                        if n < 2:
                            st.done(op)
                        else:
                            op.then_inc(conv, 1)
            st.end(TRIPS)


CH_X, CH_B, CH_C, CH_Q, CH_K, CH_V = 0, 8, 12, 16, 24, 32


def turn_stage(nc, m):
    m.vt = m.ch[:, CH_X:CH_X + 8, :].rearrange("p (t a) n -> p t (a n)", t=TT)
    m.kt = m.ch[:, CH_V:CH_V + 8, :].rearrange("p (t a) n -> p t (a n)", t=TT)
    with ExitStack() as ctx:
        work = m.region(AT_WORK, AT_END - 4.25)
        s2 = work.take("squares_of", [P, 4, T])
        rt = work.take("norms_of", [P, 4, T])
        squared, summed, rooted, dve_s = (m.sem(x) for x in ("qk_squared", "qk_summed", "qk_rooted", "qk_dve_steps"))
        scaled, turned, copied_a, copied_v = (m.sem(x) for x in ("qk_scaled", "turned", "turned_copied_act", "turned_copied_dve"))
        block = ctx.enter_context(nc.Block())
        order = [(CH_X, m.xt), (CH_V, m.vt), (CH_K, m.kt)]
        HALF = 2

        @block.vector
        def _(dve):
            st = Steps(dve, dve_s)
            for base, scale in ((CH_Q, GDN_D ** -0.5), (CH_K, 1.0)):
                with dve.Fori(0, 2) as i:
                    st.loop(i, 4)
                    k0 = 0 if base == CH_Q else 8
                    for j in range(4):
                        c = m.ch[:, bass.ds(i * 4 + (base + j), 1), :]
                        dve.tensor_tensor(s2[:, j:j + 1, :], c, c, ALU.mult).then_inc(squared, 1)
                    for j in range(4):
                        dve.wait_ge(rooted, i * 4 + (k0 + j + 1))
                        st.done(dve.reciprocal(rt[:, j, :], rt[:, j, :]))
                        c = m.ch[:, bass.ds(i * 4 + (base + j), 1), :]
                        dve.scalar_tensor_tensor(c, c, scale, rt[:, j:j + 1, :], ALU.mult, ALU.mult).then_inc(scaled, 1)
                st.end(2)
            for n, (base, out) in enumerate(order):
                for tt in range(TT):
                    g = (n * TT + tt) * HALF + 1
                    dve.wait_ge(turned, g + 1)
                    dve.tensor_copy(out[:, tt, CW:2 * CW], m.ps[:, 4 + g % 4, :]).then_inc(copied_v, 1)

        @block.tensor
        def _(pe):
            for base in (0, 8):
                with pe.Fori(0, 2) as i:
                    for j in range(4):
                        pe.wait_ge(squared, i * 4 + (base + j + 1))
                        pe.matmul(m.ps[:, j, :], sq(m, "ones"), s2[:, j, :], start=True, stop=True).then_inc(summed, 1)
            pe.wait_ge(scaled, 16)
            for n, (base, out) in enumerate(order):
                for tt in range(TT):
                    for half in range(HALF):
                        g = (n * TT + tt) * HALF + half
                        if g >= 4:
                            pe.wait_ge(copied_v if half else copied_a, g // 2 - 1)
                        for a in range(4):
                            last = pe.transpose(m.ps[:, 4 + g % 4, a * P:(a + 1) * P],
                                                m.ch[:, base + half * 4 + a, tt * P:(tt + 1) * P], sq(m, "eye"))
                        last.then_inc(turned, 1)

        @block.scalar
        def _(act):
            for base in (0, 8):
                with act.Fori(0, 2) as i:
                    for j in range(4):
                        act.wait_ge(summed, i * 4 + (base + j + 1))
                        act.activation(rt[:, j, :], m.ps[:, j, :], ACT.Sqrt, bias=m.eps[:, 0:1]).then_inc(rooted, 1)
            for n, (base, out) in enumerate(order):
                for tt in range(TT):
                    g = (n * TT + tt) * HALF
                    act.wait_ge(turned, g + 1)
                    act.activation(out[:, tt, 0:CW], m.ps[:, 4 + g % 4, :], ACT.Copy).then_inc(copied_a, 1)


def ssd_stage(nc, m):
    W4 = SSD_R * P
    with ExitStack() as ctx:
        regions = [m.region(AT_OG, AT_CH), m.region(AT_WORK, AT_END - 4.25)]
        e = [regions[1].take(f"mix{s}", [P, 2, 3, SSD_R, P]) for s in range(SEQS)]
        regions[0], regions[1] = regions[0], regions[1]
        per = lambda name, shape: [regions[s].take(f"{name}{s}", shape) for s in range(SEQS)]
        sems = lambda name: [m.sem(f"ssd_{name}{s}") for s in range(SEQS)]
        bst, steps = per("b_stage", [P, L]), per("decay_steps", [P, 3, SSD_R, P])
        sc, xd = per("masked_scores", [P, 2, 3, P]), per("x_dt", [P, 2, TS, SSD_R, SSD_P])
        staged, scored, stepped, summed, decayed = (sems(x) for x in ("staged", "scored", "steps_made", "summed", "decayed"))
        mixed, x_done, y_done, out_done = (sems(x) for x in ("mixed", "x_dt_done", "y_done", "out_done"))
        dve_s = m.sem("ssd_dve_steps")
        bank = lambda s, n: m.ps[:, 4 * s + n, :]
        block = ctx.enter_context(nc.Block())

        @block.scalar
        def _(act):
            with act.Fori(0, SSD_G) as g:
                for s in range(SEQS):
                    hold(act, m, y_done[s], g + 1)
                    act.activation(bst[s][:, :], m.ch[:, bass.ds(g + CH_B, 1), s * L:(s + 1) * L], ACT.Copy).then_inc(staged[s], 1)
                for d in range(2):
                    for s in range(SEQS):
                        act.wait_ge(summed[s], g * 2 + (d + 2))
                        for b in range(3):
                            last = act.activation(e[s][:, d, b, :, :].rearrange("p h c -> p (h c)"), bank(s, 1 + b), ACT.Exp)
                        last.then_inc(decayed[s], 1)

        @block.gpsimd
        def _(pool):
            with pool.Fori(0, SSD_G) as g:
                for d in range(2):
                    mask = sq(m, "ge" if d else "le").unsqueeze(1).broadcast_to([P, SSD_R, P])
                    for s in range(SEQS):
                        hold(pool, m, summed[s], g * 2 + (d + 1))
                        for t in range(TS):
                            col = m.decay[:, TS * s + t, bass.ds(g * SSD_R + d * SSD_H, SSD_R)].unsqueeze(2)
                            pool.tensor_tensor(steps[s][:, t, :, :], col.broadcast_to([P, SSD_R, P]), mask, ALU.mult)
                        col = m.decay[:, TS * s + d, bass.ds(g * SSD_R + d * SSD_H, SSD_R)].unsqueeze(2)
                        pool.tensor_copy(steps[s][:, 2, :, :], col.broadcast_to([P, SSD_R, P])).then_inc(stepped[s], 1)

        @block.tensor
        def _(pe):
            for s in range(SEQS):
                pe.sem_inc(summed[s], 1)
                pe.sem_inc(y_done[s], 1)
            with pe.Fori(0, SSD_G) as g:
                for s in range(SEQS):
                    pe.wait_ge(staged[s], g + 1)
                    pe.wait_ge(out_done[s], g + 1)
                    for t in range(TS):
                        last = pe.matmul(bank(s, 0)[:, t * L:(t + 1) * L], bst[s][:, t * P:(t + 1) * P],
                                         m.ch[:, bass.ds(g + CH_C, 1), s * L:(s + 1) * L], start=True, stop=True)
                    last.then_inc(scored[s], 1)
                for d in range(2):
                    before = "lt" if d else "gt"
                    for s in range(SEQS):
                        pe.wait_ge(stepped[s], g * 2 + (d + 1))
                        pe.wait_ge(decayed[s], g * 2 + (d + 1))
                        rhs = [steps[s][:, n, :, :].rearrange("p h c -> p (h c)") for n in range(3)]
                        pe.matmul(bank(s, 1), sq(m, before), rhs[0], start=True, stop=True)
                        pe.matmul(bank(s, 3), sq(m, before), rhs[1], start=True, stop=True)
                        pe.matmul(bank(s, 2), sq(m, before), rhs[2], start=True, stop=False)
                        pe.matmul(bank(s, 2), sq(m, "ones"), rhs[1 - d], start=False, stop=True).then_inc(summed[s], 1)
                for s in range(SEQS):
                    pe.wait_ge(mixed[s], g * 2 + 2)
                    pe.wait_ge(x_done[s], g + 1)
                    for t in range(TS):
                        terms = [(0, 2 * t, t), (1, 2 * t, t), ((0, 1, 0) if t else (1, 1, 1))]
                        for h in range(SSD_R):
                            o = bank(s, 0)[:, (t * SSD_R + h) * SSD_P:(t * SSD_R + h + 1) * SSD_P]
                            for n, (d, b, src) in enumerate(terms):
                                last = pe.matmul(o, e[s][:, d, b, h, :], xd[s][:, d, src, h, :], start=n == 0, stop=n == 2)
                    last.then_inc(y_done[s], 1)

        @block.vector
        def _(dve):
            st = Steps(dve, dve_s)
            for s in range(SEQS):
                dve.sem_inc(out_done[s], 1)
                dve.sem_inc(decayed[s], 1)
            with dve.Fori(0, SSD_G) as g:
                st.loop(g, 2 * SEQS)
                xs = [m.xt[:, TS * s:TS * s + TS, bass.ds(g * (SSD_R * SSD_P), SSD_R * SSD_P)]
                      .rearrange("p t (h c) -> p t h c", c=SSD_P) for s in range(SEQS)]
                for s in range(SEQS):
                    dve.wait_ge(scored[s], g + 1)
                    le, ge = sq(m, "le"), sq(m, "ge")
                    blk = lambda src, dst: bank(s, 0)[:, src * L + dst * P:src * L + dst * P + P]
                    for t in range(TS):
                        dve.tensor_tensor(sc[s][:, 0, 2 * t, :], blk(t, t), le, ALU.mult)
                        dve.tensor_tensor(sc[s][:, 1, 2 * t, :], blk(t, t), ge, ALU.mult)
                    dve.tensor_copy(sc[s][:, 0, 1, :], blk(0, 1))
                    st.done(dve.tensor_copy(sc[s][:, 1, 1, :], blk(1, 0)))
                    dve.wait_ge(y_done[s], g + 1)
                    for d in range(2):
                        dt = m.small[:, TS * s:TS * s + TS, bass.ds(g * SSD_R + d * SSD_H, SSD_R)].unsqueeze(3)
                        last = dve.tensor_tensor(xd[s][:, d, :, :, :], xs[s], dt.broadcast_to([P, TS, SSD_R, SSD_P]), ALU.mult)
                    last.then_inc(x_done[s], 1)
                for d in range(2):
                    for s in range(SEQS):
                        dve.wait_ge(decayed[s], g * 2 + (d + 2))
                        for b in range(3):
                            last = dve.tensor_tensor(e[s][:, d, b, :, :], e[s][:, d, b, :, :],
                                                     sc[s][:, d, b, :].unsqueeze(1).broadcast_to([P, SSD_R, P]), ALU.mult)
                        last.then_inc(mixed[s], 1)
                for s in range(SEQS):
                    skip = m.rowp[:, bass.ds(g * SSD_R + ROW_D, SSD_R)].unsqueeze(1).unsqueeze(3)
                    st.done(dve.tensor_tensor(xs[s], xs[s], skip.broadcast_to([P, TS, SSD_R, SSD_P]), ALU.mult))
                    dve.wait_ge(y_done[s], g + 2)
                    y = bank(s, 0).rearrange("p (t h c) -> p t h c", t=TS, h=SSD_R)
                    dve.tensor_tensor(xs[s], y, xs[s], ALU.add).then_inc(out_done[s], 1)
            st.end(SSD_G)


def gdn_stage(nc, m):
    NL = len(LEVELS)
    with ExitStack() as ctx:
        spare = m.region(AT_CH + 2 * CH_B, AT_CH + 2 * CH_Q)
        work = m.region(AT_WORK, AT_END - 4.25)

        def per(name, shape):
            size = 4 * int(np.prod(shape[1:]))
            return [(spare if spare.at + size <= spare.end else work).take(f"gdn_{name}{s}", shape) for s in range(SEQS)]

        sems = lambda name: [m.sem(f"gdn_{name}{s}") for s in range(SEQS)]
        kq = per("kq", [P, 2, L])
        steps, e, at, qk = (per(x, [P, 2, 2, P]) for x in ("steps", "decay", "a_t", "qk"))
        am, y, inv, invt = (per(x, [P, 4, P]) for x in ("a_level", "y", "inv", "inv_t"))
        vn, kd, st8, z, oq = per("v_new", [P, 4, P]), per("k_dec", [P, 2, P]), per("state", [P, 2, P]), per("z", [P, 2, P]), per("o_state", [P, 2, P])
        (staged, kq_done, stepped, summed, decayed, weighed, a_made, levelled, inv_done, turned, copied, y_done, y_copied,
         p_done, u_done, vn_done, kd_done, s_done, s_copied, ks_done, z_done, w_done, o_done, out_done) = (
            sems(x) for x in ("staged", "kq", "steps_made", "summed", "decayed", "weighed", "a_made", "levelled",
                              "inv_t_done", "inv_turned", "inv_copied", "y_done", "y_copied", "p_done", "tv_done", "v_new_done", "k_dec_done",
                              "state_done", "state_copied", "ks_done", "z_done", "tz_done", "o_done", "out_done"))
        dve_s = m.sem("gdn_dve_steps")
        bank = lambda s, n: m.ps[:, 4 * s + n, :]
        bank4 = lambda s, n: m.ps[:, 4 * s + n, :].rearrange("p (i c) -> p i c", c=P)
        first = (0, 3)
        second = (1, 2)
        col = lambda h, d: bass.ds(h + d * GDN_H, 1)
        block = ctx.enter_context(nc.Block())

        @block.scalar
        def _(act):
            for s in range(SEQS):
                act.sem_inc(decayed[s], 1)
            with act.Fori(0, GDN_H) as h:
                for s in range(SEQS):
                    hold(act, m, o_done[s], h + 1)
                    for n, base in enumerate((CH_K, CH_Q)):
                        last = act.activation(kq[s][:, n:n + 1, :], m.ch[:, bass.ds(h + base, 1), s * L:(s + 1) * L], ACT.Copy)
                    last.then_inc(staged[s], 1)
                for s in range(SEQS):
                    for n, i in enumerate(first):
                        scale = m.edk[:, 2 + n, TS * s + i % 2, col(h, n)]
                        last = act.activation(kd[s][:, n, :], m.kt[:, TS * s + i % 2, bass.ds(h * P, P)], ACT.Copy, scale=scale)
                    last.then_inc(kd_done[s], 1)
                for s in range(SEQS):
                    act.wait_ge(summed[s], h + 1)
                    act.activation(e[s][:, :, :, :].rearrange("p d c n -> p (d c n)"), bank(s, 1), ACT.Exp).then_inc(decayed[s], 1)
                for lv in range(NL):
                    for s in range(SEQS):
                        act.wait_ge(turned[s], h * NL + (lv + 1))
                        act.activation(inv[s][:, :, :], bank4(s, 1), ACT.Copy).then_inc(copied[s], 1)
                    for s in range(SEQS):
                        act.wait_ge(y_done[s], h * NL + (lv + 1))
                        act.activation(y[s][:, :, :], bank4(s, 2), ACT.Copy).then_inc(y_copied[s], 1)
                for s in range(SEQS):
                    act.wait_ge(s_done[s], h + 1)
                    act.activation(st8[s][:, :, :], bank4(s, 2)[:, 0:2, :], ACT.Copy).then_inc(s_copied[s], 1)

        @block.gpsimd
        def _(pool):
            with pool.Fori(0, GDN_H) as h:
                for s in range(SEQS):
                    hold(pool, m, decayed[s], h + 1)
                    for d in range(2):
                        g = m.decay[:, TS * s:TS * s + TS, bass.ds(h + (32 + d * GDN_H), 1)].broadcast_to([P, TS, P])
                        mask = sq(m, "ge" if d else "le").unsqueeze(1).broadcast_to([P, TS, P])
                        last = pool.tensor_tensor(steps[s][:, d, :, :], g, mask, ALU.mult)
                    last.then_inc(stepped[s], 1)
                for lv, b in enumerate((1,) + LEVELS):
                    mask = sq(m, f"lvl{b}").unsqueeze(1).broadcast_to([P, 4, P])
                    for s in range(SEQS):
                        if lv == 0:
                            pool.wait_ge(a_made[s], h + 1)
                        elif lv == 1:
                            pool.wait_ge(inv_done[s], h * (NL + 1) + 1)
                        else:
                            pool.wait_ge(y_done[s], h * NL + (lv - 1))
                        pool.tensor_tensor(am[s][:, :, :], at[s][:, :, :, :].rearrange("p d c n -> p (d c) n"), mask,
                                           ALU.mult).then_inc(levelled[s], 1)

        @block.vector
        def _(dve):
            st = Steps(dve, dve_s)
            for s in range(SEQS):
                dve.sem_inc(out_done[s], 1)
            with dve.Fori(0, GDN_H) as h:
                st.loop(h, SEQS)
                for s in range(SEQS):
                    dve.wait_ge(decayed[s], h + 2)
                    strict, incl = sq_pair(m, "lt", 2), sq_pair(m, "le", 2)
                    dve.tensor_tensor(qk[s][:, :, :, :], e[s][:, :, :, :], incl, ALU.mult)
                    st.done(dve.tensor_tensor(e[s][:, :, :, :], e[s][:, :, :, :], strict, ALU.mult))
                    dve.wait_ge(kq_done[s], h + 1)
                    kk = bank(s, 0).rearrange("p (c a n) -> p c a n", c=2, a=2)
                    for d in range(2):
                        for c in range(TS):
                            beta = m.small[:, TS * s + c, bass.ds(h + (48 + d * GDN_H), 1)]
                            last = dve.scalar_tensor_tensor(at[s][:, d, c, :], e[s][:, d, c, :], beta, kk[:, c, 0, :],
                                                            ALU.mult, ALU.mult)
                    last.then_inc(a_made[s], 1)
                    for d in range(2):
                        last = dve.tensor_tensor(qk[s][:, d, :, :], qk[s][:, d, :, :], kk[:, :, 1, :], ALU.mult)
                    last.then_inc(weighed[s], 1)
                for s in range(SEQS):
                    dve.wait_ge(levelled[s], h * (NL + 1) + 1)
                    dve.tensor_tensor(invt[s][:, :, :], sq(m, "eye").unsqueeze(1).broadcast_to([P, 4, P]), am[s][:, :, :],
                                      ALU.subtract).then_inc(inv_done[s], 1)
                for lv in range(NL):
                    for s in range(SEQS):
                        dve.wait_ge(p_done[s], h * NL + (lv + 1))
                        dve.tensor_tensor(invt[s][:, :, :], invt[s][:, :, :], bank4(s, 3), ALU.subtract).then_inc(inv_done[s], 1)
                for s in range(SEQS):
                    dve.wait_ge(u_done[s], h + 1)
                    for n, i in enumerate(first):
                        beta = m.small[:, TS * s + i % 2, bass.ds(h + (48 + n * GDN_H), 1)]
                        last = dve.tensor_scalar(vn[s][:, i, :], bank4(s, 3)[:, n, :], beta, None, ALU.mult)
                    last.then_inc(vn_done[s], 1)
                for s in range(SEQS):
                    dve.wait_ge(ks_done[s], h + 1)
                    for n, i in enumerate(second):
                        t = TS * s + i % 2
                        ks = bank4(s, 1)
                        dve.scalar_tensor_tensor(z[s][:, n, :], ks[:, 2 * n, :], m.ned[:, n, t, col(h, n)],
                                                 m.vt[:, t, bass.ds(h * P, P)], ALU.mult, ALU.add)
                        last = dve.tensor_scalar(oq[s][:, i % 2, :], ks[:, 2 * n + 1, :], m.edk[:, n, t, col(h, n)], None, ALU.mult)
                    last.then_inc(z_done[s], 1)
                for s in range(SEQS):
                    dve.wait_ge(w_done[s], h + 1)
                    for n, i in enumerate(second):
                        beta = m.small[:, TS * s + i % 2, bass.ds(h + (48 + n * GDN_H), 1)]
                        last = dve.tensor_scalar(vn[s][:, i, :], bank4(s, 3)[:, 2 + n, :], beta, None, ALU.mult)
                    last.then_inc(vn_done[s], 1)
                for s in range(SEQS):
                    dve.wait_ge(o_done[s], h + 2)
                    dve.tensor_tensor(m.og[:, TS * s:TS * s + TS, bass.ds(h * P, P)], bank4(s, 0)[:, 0:2, :], oq[s][:, :, :],
                                      ALU.add).then_inc(out_done[s], 1)
            st.end(GDN_H)

        @block.tensor
        def _(pe):
            for s in range(SEQS):
                pe.sem_inc(o_done[s], 1)
            with pe.Fori(0, GDN_H) as h:
                for s in range(SEQS):
                    pe.wait_ge(staged[s], h + 1)
                    pe.wait_ge(out_done[s], h + 1)
                    for c in range(TS):
                        last = pe.matmul(bank(s, 0)[:, c * L:(c + 1) * L].rearrange("p (a n) -> p a n", a=2),
                                         kq[s][:, 0, c * P:(c + 1) * P], kq[s][:, :, c * P:(c + 1) * P], start=True, stop=True)
                    last.then_inc(kq_done[s], 1)
                for s in range(SEQS):
                    pe.wait_ge(stepped[s], h + 1)
                    for d in range(2):
                        last = pe.matmul(bank(s, 1)[:, d * L:(d + 1) * L], sq(m, "lt" if d else "gt"),
                                         steps[s][:, d, :, :].rearrange("p c n -> p (c n)"), start=True, stop=True)
                    last.then_inc(summed[s], 1)

                def turn(s, lv):
                    pe.wait_ge(inv_done[s], h * (NL + 1) + (lv + 1))
                    for i in range(4):
                        last = pe.transpose(bank4(s, 1)[:, i, :], invt[s][:, i, :], sq(m, "eye"))
                    last.then_inc(turned[s], 1)

                for s in range(SEQS):
                    turn(s, 0)
                for lv in range(NL):
                    for s in range(SEQS):
                        pe.wait_ge(copied[s], h * NL + (lv + 1))
                        pe.wait_ge(levelled[s], h * (NL + 1) + (lv + 2))
                        for i in range(4):
                            last = pe.matmul(bank4(s, 2)[:, i, :], am[s][:, i, :], inv[s][:, i, :], start=True, stop=True)
                        last.then_inc(y_done[s], 1)
                    for s in range(SEQS):
                        pe.wait_ge(y_copied[s], h * NL + (lv + 1))
                        for i in range(4):
                            last = pe.matmul(bank4(s, 3)[:, i, :], y[s][:, i, :], invt[s][:, i, :], start=True, stop=True)
                        last.then_inc(p_done[s], 1)
                    if lv < NL - 1:
                        for s in range(SEQS):
                            turn(s, lv + 1)
                v = lambda s, i: m.vt[:, TS * s + i % 2, bass.ds(h * P, P)]
                for s in range(SEQS):
                    pe.wait_ge(inv_done[s], (h + 1) * (NL + 1))
                    for n, i in enumerate(first):
                        last = pe.matmul(bank4(s, 3)[:, n, :], invt[s][:, i, :], v(s, i), start=True, stop=True)
                    last.then_inc(u_done[s], 1)
                for s in range(SEQS):
                    pe.wait_ge(vn_done[s], h * 2 + 1)
                    pe.wait_ge(kd_done[s], h + 1)
                    for n, i in enumerate(first):
                        last = pe.matmul(bank4(s, 2)[:, n, :], kd[s][:, n, :], vn[s][:, i, :], start=True, stop=True)
                    last.then_inc(s_done[s], 1)
                for s in range(SEQS):
                    pe.wait_ge(s_copied[s], h + 1)
                    for n, i in enumerate(second):
                        c = i % 2
                        for a in range(2):
                            last = pe.matmul(bank4(s, 1)[:, 2 * n + a, :], kq[s][:, a, c * P:(c + 1) * P], st8[s][:, n, :],
                                             start=True, stop=True)
                    last.then_inc(ks_done[s], 1)
                for s in range(SEQS):
                    pe.wait_ge(z_done[s], h + 1)
                    for n, i in enumerate(second):
                        last = pe.matmul(bank4(s, 3)[:, 2 + n, :], invt[s][:, i, :], z[s][:, n, :], start=True, stop=True)
                    last.then_inc(w_done[s], 1)
                for s in range(SEQS):
                    pe.wait_ge(vn_done[s], h * 2 + 2)
                    pe.wait_ge(weighed[s], h + 1)
                    for c in range(TS):
                        for d in range(2):
                            last = pe.matmul(bank4(s, 0)[:, c, :], qk[s][:, d, c, :], vn[s][:, 2 * d + c, :], start=d == 0, stop=d == 1)
                    last.then_inc(o_done[s], 1)


class Stream:

    def __init__(self, m, raw, split, tag, chunks):
        self.m, self.chunks = m, chunks
        self.w = raw.take(f"{tag}_slots", [P, 2, KT // 2, CW])
        self.wh = split.take(f"{tag}_high", [P, 2, KT // 2, CW], F32R)
        self.wl = split.take(f"{tag}_low", [P, 2, KT // 2, CW], F32R)
        self.loaded = [m.sem(f"{tag}_slot{j}_loaded") for j in range(2)]
        self.high_done, self.low_done, self.used, self.prod = (m.sem(f"{tag}_{x}") for x in ("high", "low", "first_half_used", "products"))

    def sp(self, sp):
        for n in range(2 * len(self.chunks)):
            j, half = n % 2, KT // 2 * CW
            if n >= 2:
                sp.wait_ge(self.low_done, n - 1)
            src = self.chunks[n // 2][:, j * half:(j + 1) * half]
            sp.dma_start(self.w[:, j, :, :], src.rearrange("p (k n) -> p k n", n=CW)).then_inc(self.loaded[j], 16)

    def high(self, act, n):
        if n >= 2 * len(self.chunks):
            return
        j, pair = n % 2, n // 2
        act.wait_ge(self.loaded[j], 16 * (pair + 1))
        if pair:
            act.wait_ge(self.prod if j else self.used, 4 * pair if j else pair)
        act.activation(self.wh[:, j, :, :], self.w[:, j, :, :], ACT.Copy).then_inc(self.high_done, 1)

    def pool(self, pool):
        for n in range(2 * len(self.chunks)):
            j = n % 2
            pool.wait_ge(self.high_done, n + 1)
            pool.tensor_tensor(self.wl[:, j, :, :], self.w[:, j, :, :], bits32(self.wh[:, j, :, :]),
                               ALU.subtract).then_inc(self.low_done, 1)

    def act(self, act, pair, consume):
        self.high(act, 2 * pair + 2)
        consume()
        self.high(act, 2 * pair + 3)

    def pe(self, pe, pair, banks, free, x, token_major):
        m = self.m
        for j in range(2):
            pe.wait_ge(self.low_done, 2 * pair + j + 1)
            for f in range(4):
                if j == 0:
                    free(f)
                c = slice(f * P, (f + 1) * P)
                for k in range(KT // 2):
                    kt = j * (KT // 2) + k
                    if token_major:
                        a, b = [y[:, kt, c] for y in x], [w[:, j, k, :] for w in (self.wh, self.wl)]
                    else:
                        a, b = [w[:, j, k, c] for w in (self.wh, self.wl)], [y[:, kt, :] for y in x]
                    for n, (u, v) in enumerate(((0, 0), (0, 1), (1, 0))):
                        last = pe.matmul(m.ps[:, banks + f, :], a[u], b[v], start=kt == 0 and n == 0,
                                         stop=kt == KT - 1 and n == 2)
                if j:
                    last.then_inc(self.prod, 1)
            if j == 0:
                last.then_inc(self.used, 1)


def merge_stage(nc, m):
    G = (SSD_G, GDN_H)
    chunks = [m.ins["w_gates"][n] for n in (0, 1, 4, 5)]
    for a, name in enumerate(("w_ssd_out", "w_gdn_out")):
        for n in range(2):
            chunks += [m.ins[name][n], m.ins["w_gates"][4 * a + 2 + n]]
    chunks += [m.ins["w_out"][n] for n in range(2)]
    y = (m.xt, m.og)
    over = m.region(AT_XT, AT_CH)
    mh, ml = over.take("merged_high", [P, KT, T], F32R), over.take("merged_low", [P, KT, T], F32R)
    r = m.region(AT_CH, AT_END)
    yh, yl = r.take("mixer_high", [P, KT, T], F32R), r.take("mixer_low", [P, KT, T], F32R)
    mT = r.take("merged", [P, KT, T])
    zt = r.take("silu_z", [P, 4, CW])
    sqs = r.take("mixer_squares", [P, 2, D])
    sg = r.take("sig_gate", [P, 4, CW])
    ss = r.take("mixer_stat", [P, 2, TT, 8])
    stream = Stream(m, r, r, "merge", chunks)
    prod = stream.prod
    (silu, gated, squared, reduced, meaned, rooted, dve_s, scaled, turned, t_high, t_out, sig, mixed, m_high, m_low, added) = (
        m.sem(f"merge_{x}") for x in ("silu", "z_multiplied", "squared", "reduced", "meaned", "rooted", "dve_steps", "scaled",
                                      "turned", "turned_high", "turned_low", "gate_sigmoid", "mixed", "merged_high",
                                      "merged_low", "added"))
    n_x = (m.nh, m.nl)
    FIRST = (4, 8)
    with nc.Block() as block:

        @block.sync
        def _(sp):
            stream.sp(sp)

        @block.gpsimd
        def _(pool):
            stream.pool(pool)

        @block.tensor
        def _(pe):
            for p in range(4):
                stream.pe(pe, p, 4 * (p % 2), lambda tt: p < 2 or pe.wait_ge(silu, 4 * (p - 2) + tt + 1), n_x, True)
            for a in range(2):
                for kt in range(KT):
                    if a == 0:
                        pe.wait_ge(silu, 9 + kt)
                    elif kt == 0:
                        pe.wait_ge(mixed, 8)
                    if kt == 0:
                        pe.wait_ge(scaled, TT * (a + 1))
                    for tt in range(TT):
                        last = pe.transpose(m.ps[:, kt, tt * P:(tt + 1) * P], y[a][:, tt, kt * P:(kt + 1) * P], sq(m, "eye"))
                    last.then_inc(turned, 1)
                for n in range(2):
                    for gate in range(2):
                        p = FIRST[a] + 2 * n + gate

                        def free(f):
                            if n == 0:
                                pe.wait_ge(t_out, KT * a + (KT if gate == 0 and f == 0 else 4 * gate + f + 1))
                            else:
                                pe.wait_ge(sig if gate else mixed, 4 * (2 * a) + f + 1)
                        stream.pe(pe, p, 4 * gate, free, n_x if gate else (yh, yl), False)

            def free_out(tt, p):
                if tt == 0:
                    pe.wait_ge(m_low, KT)
                if p == 13:
                    pe.wait_ge(sig, 16)
            for p in (12, 13):
                stream.pe(pe, p, 4 * (p - 12), lambda tt: free_out(tt, p), (mh, ml), True)

        @block.scalar
        def _(act):
            def squares(a, first):
                for tt in range(TT):
                    n = first + tt
                    if n >= 2:
                        act.wait_ge(reduced, n - 1)
                    act.activation(sqs[:, tt % 2, :], y[a][:, tt, :], ACT.Square).then_inc(squared, 1)

            def z(p):
                for tt in range(TT):
                    g = 4 * p + tt
                    act.wait_ge(prod, g + 1)
                    if g >= 4:
                        act.wait_ge(gated, g - 3)
                    act.activation(zt[:, tt, :], m.ps[:, 4 * (p % 2) + tt, :], ACT.Silu).then_inc(silu, 1)

            def sigmoids(p, k):
                for f in range(4):
                    act.wait_ge(prod, 4 * p + f + 1)
                    if k:
                        act.wait_ge(mixed, 4 * (k - 1) + f + 1)
                    act.activation(sg[:, f, :], m.ps[:, 4 + f, :], ACT.Sigmoid).then_inc(sig, 1)

            stream.high(act, 0)
            stream.high(act, 1)
            squares(1, 0)
            for p in range(2):
                stream.act(act, p, lambda: z(p))
            act.wait_ge(gated, 8)
            squares(0, TT)
            act.wait_ge(meaned, 1)
            act.activation(ss[:, :, :, :], ss[:, :, :, :], ACT.Sqrt).then_inc(rooted, 1)
            for p in range(2, 4):
                stream.act(act, p, lambda: z(p))
            for a in range(2):
                for kt in range(KT):
                    act.wait_ge(turned, KT * a + kt + 1)
                    col = COL_GDNN if a else COL_SSDN + kt
                    act.activation(yh[:, kt, :], m.ps[:, kt, :], ACT.Copy, scale=m.colp[:, col:col + 1]).then_inc(t_high, 1)
                for n in range(2):
                    p = FIRST[a] + 2 * n
                    stream.act(act, p, lambda: None)
                    stream.act(act, p + 1, lambda: sigmoids(p + 1, 2 * a + n))
                    if a:
                        for f in range(4):
                            act.wait_ge(mixed, 8 + 4 * n + f + 1)
                            act.activation(mh[:, 4 * n + f, :], mT[:, 4 * n + f, :], ACT.Copy).then_inc(m_high, 1)
            stream.act(act, 12, lambda: None)

        @block.vector
        def _(dve):
            st = Steps(dve, dve_s)

            def reduce(a, first):
                for tt in range(TT):
                    dve.wait_ge(squared, first + tt + 1)
                    dve.tensor_reduce(ss[:, a, tt, 0:G[a]], sqs[:, tt % 2, :].rearrange("p (g c) -> p g c", g=G[a]),
                                      AX.X, ALU.add).then_inc(reduced, 1)

            def times_z(a):
                for g in range(8 * a, 8 * a + 8):
                    dve.wait_ge(silu, g + 1)
                    n = (g // 4) % 2
                    v = y[a][:, g % 4, n * CW:(n + 1) * CW]
                    dve.tensor_tensor(v, v, zt[:, g % 4, :], ALU.mult).then_inc(gated, 1)

            def scale(a):
                dve.wait_ge(gated, 8 * (a + 1))
                for tt in range(TT):
                    v = y[a][:, tt, :].rearrange("p (g c) -> p g c", g=G[a])
                    dve.tensor_tensor(v, v, ss[:, a, tt, 0:G[a]].unsqueeze(2).broadcast_to([P, G[a], D // G[a]]),
                                      ALU.mult).then_inc(scaled, 1)

            st.done(dve.memset(ss[:, :, :, :], 1.0))
            reduce(1, 0)
            times_z(0)
            reduce(0, TT)
            dve.wait_ge(reduced, 2 * TT)
            for a in range(2):
                last = dve.tensor_scalar(ss[:, a, :, 0:G[a]], ss[:, a, :, 0:G[a]], G[a] / D, EPS, ALU.mult, ALU.add)
            last.then_inc(meaned, 1)
            dve.wait_ge(rooted, 1)
            st.done(dve.reciprocal(ss[:, :, :, :], ss[:, :, :, :]))
            scale(0)
            times_z(1)
            scale(1)
            for a in range(2):
                for kt in range(KT):
                    dve.wait_ge(t_high, KT * a + kt + 1)
                    col = COL_GDNN if a else COL_SSDN + kt
                    dve.scalar_tensor_tensor(yl[:, kt, :], m.ps[:, kt, :], m.colp[:, col:col + 1], bits32(yh[:, kt, :]),
                                             ALU.mult, ALU.subtract).then_inc(t_out, 1)
                for n in range(2):
                    for f in range(4):
                        o = mT[:, 4 * n + f, :]
                        dve.wait_ge(sig, 4 * (2 * a + n) + f + 1)
                        if a == 0:
                            dve.tensor_tensor(o, m.ps[:, f, :], sg[:, f, :], ALU.mult).then_inc(mixed, 1)
                        else:
                            st.done(dve.tensor_tensor(sg[:, f, :], m.ps[:, f, :], sg[:, f, :], ALU.mult))
                            dve.tensor_tensor(o, o, sg[:, f, :], ALU.add).then_inc(mixed, 1)
                    if a:
                        for f in range(4):
                            dve.wait_ge(m_high, 4 * n + f + 1)
                            dve.tensor_tensor(ml[:, 4 * n + f, :], mT[:, 4 * n + f, :], bits32(mh[:, 4 * n + f, :]),
                                              ALU.subtract).then_inc(m_low, 1)
            for n in range(2):
                for tt in range(TT):
                    dve.wait_ge(prod, 4 * (12 + n) + tt + 1)
                    v = m.h[:, tt, n * CW:(n + 1) * CW]
                    dve.tensor_tensor(v, v, m.ps[:, 4 * n + tt, :], ALU.add).then_inc(added, 1)


def expert_stages(nc, m, last_stage):
    g_dense = nc.dram_tensor("g_dense", (PEER_K, P, T), F32, kind="Internal").ap()
    a_dense = nc.dram_tensor("a_dense", (PEER_K, P, T), F32, kind="Internal").ap()
    m.scores = m.region(AT_SCORES, AT_SCORES + 32).take("key_scores", [P, TT, NHZ, PEER_K])
    down = DownLoads(nc, m, g_dense, a_dense)
    for n, (stage, args) in enumerate(((query_stage, ()), (up_stage, (g_dense, a_dense, down)), (down_stage, (down,)))):
        if last_stage > 2 + n * 0.1:
            stage(nc, m, *args)
            end_stage(nc, m)


def query_stage(nc, m):
    r = m.region(AT_SCORES + 32, AT_END)
    norm = NormT(nc, m, r, "ffn_norm", COL_FFN)
    qT = r.take("queries", [P, NHZ, T])
    keys = r.take("keys", [P, NHZ, PEER_K])
    q_out, scored, s_out, keys_in = (m.sem(f"query_{x}") for x in ("copied", "scored", "scores_out", "keys_in"))
    stream = Stream(m, r, r, "query", [m.ins["peer_query"][n] for n in range(4)])
    with nc.Block() as block:

        @block.sync
        def _(sp):
            sp.dma_start(keys[:, :, :], m.ins["peer_keys"].rearrange("p (a k) -> p a k", k=PEER_K)).then_inc(keys_in, 16)
            stream.sp(sp)

        @block.gpsimd
        def _(pool):
            stream.pool(pool)

        @block.tensor
        def _(pe):
            norm.pe(pe)
            pe.wait_ge(norm.out_done, KT)
            for p in range(4):
                stream.pe(pe, p, 4 * (p % 2), lambda f: p < 2 or pe.wait_ge(q_out, 4 * (p - 2) + f + 1), (m.nh, m.nl), False)
            pe.wait_ge(keys_in, 16)
            pe.wait_ge(q_out, NHZ)
            for g in range(4 * TT):
                if g >= 8:
                    pe.wait_ge(s_out, g - 7)
                for a in range(4):
                    hz = 4 * (g % 4) + a
                    last = pe.matmul(m.ps[:, g % 8, a * P:(a + 1) * P], qT[:, hz, (g // 4) * P:(g // 4 + 1) * P], keys[:, hz, :],
                                     start=True, stop=True)
                last.then_inc(scored, 1)

        @block.scalar
        def _(act):
            stream.high(act, 0)
            stream.high(act, 1)
            norm.act(act)

            def copies(p):
                for f in range(4):
                    g = 4 * p + f
                    act.wait_ge(stream.prod, g + 1)
                    act.activation(qT[:, g, :], m.ps[:, g % 8, :], ACT.Copy).then_inc(q_out, 1)

            for p in range(4):
                stream.act(act, p, lambda: copies(p))

        @block.vector
        def _(dve):
            norm.dve(dve)
            for g in range(4 * TT):
                dve.wait_ge(scored, g + 1)
                dve.tensor_copy(m.scores[:, g // 4, 4 * (g % 4):4 * (g % 4) + 4, :].rearrange("p a k -> p (a k)"),
                                m.ps[:, g % 8, :]).then_inc(s_out, 1)


def up_stage(nc, m, g_dense, a_dense, down):
    STEP = 16
    FOURS = STEP // 4
    WITH = P // STEP
    ALONE = 16
    NJ = ALONE + WITH
    PIECES = 8
    TAIL = PEER_K - TT * NJ
    r = m.region(AT_SCORES + 32, AT_END - KB_GATES)
    take = lambda name, shape, dt=F32: r.take(f"up_{name}", shape, dt)
    u, uh, ul = take("u", [P, 2, KT, P]), take("u_high", [P, 2, KT, P], F32R), take("u_low", [P, 2, KT, P], F32R)
    av = take("gelu", [P, 2, T])
    spare = take("spare", [P, NHZ * PEER_K])
    top_v, top_i, top_f = take("top_v", [P, NHZ, TOPK]), take("top_i", [P, NHZ, TOPK], U32), take("top_f", [P, NHZ, TOPK])
    best, pos, part = take("best", [P, PEER_H, TOPK]), take("pos", [P, PEER_H, TOPK], U32), take("part", [P, HK], U32)
    part_f, sums = take("part_f", [P, HK]), take("sums", [P, PEER_H])
    chosen = take("chosen", [P, 3, HK])
    high_t = take("chosen_t", [P, 3, P])
    gate_h, gate_l = take("gate_high", [P, P], F32R), take("gate_low", [P, P])
    hot_i, hot_h, hot_l = (take(f"hot_{x}", [P, STEP, P], F32R) for x in ("first", "high", "low"))
    r = m.region(AT_END - KB_GATES, AT_END)
    gs = take("gates", [P, PEER_K, P])
    sem = lambda name: m.sem(f"up_{name}")
    dve_s, exped, made, turned, t_copied, second_eq, second_low, second_high, spread, gs_done, maxed = (
        sem(x) for x in ("dve_steps", "gate_exp", "gates_made", "turned", "turned_copied", "second_key_found", "gates_low_placed",
                         "gates_high_placed", "spread", "gates_copied", "best_less_max"))
    stored = sem("gates_stored")
    u_in, a_stored = [sem(f"u{n}_loaded") for n in range(2)], [sem(f"gelu{n}_stored") for n in range(2)]
    high, low, prod, gelu = sem("u_high_done"), sem("u_low_done"), sem("products"), sem("gelu_done")
    eu = m.ins["expert_u"]
    with nc.Block() as block:

        @block.sync
        def _(sp):
            for n in range(2):
                sp.sem_inc(a_stored[n], 16)
                sp.dma_start(u[:, n, :, :].rearrange("p k i -> p (k i)"), eu[n]).then_inc(u_in[n], 16)

            def key(j, n, load=True):
                if load:
                    sp.wait_ge(low, j + 1)
                    sp.dma_start(u[:, n, :, :].rearrange("p k i -> p (k i)"),
                                 eu[bass.ds(j + 2, 1)].rearrange("a p k -> p (a k)")).then_inc(u_in[n], 16)
                sp.wait_ge(gelu, j + 3)
                sp.dma_start(a_dense[bass.ds(j, 1)].rearrange("a i t -> i (a t)"), av[:, n, :]).then_inc(a_stored[n], 16)

            def gates_piece(tt, n):
                j = slice(n * (PEER_K // PIECES), (n + 1) * (PEER_K // PIECES))
                sp.dma_start(g_dense[j, :, tt * P:(tt + 1) * P].rearrange("j i t -> i j t"), gs[:, j, :]).then_inc(stored, 16)

            for tt in range(TT):
                if tt:
                    sp.wait_ge(gs_done, tt * (P // 4) + FOURS)
                    for n in range(PIECES):
                        key(tt * NJ + n, n % 2)
                        gates_piece(tt - 1, n)
                with sp.Fori(PIECES // 2 if tt else 0, NJ // 2) as i:
                    for n in range(2):
                        key(i * 2 + (tt * NJ + n), n)
            for n in range(TAIL):
                if n == 0:
                    sp.wait_ge(gs_done, TT * (P // 4) + FOURS)
                j = PEER_K - TAIL + n
                key(j, j % 2, j < PEER_K - 2)
                if n < PIECES:
                    gates_piece(TT - 1, n)
                if n == PIECES + 2:
                    sp.wait_ge(stored, 16 * PIECES * TT)
                    for b in range(2):
                        sp.wait_ge(a_stored[b], 16 * (DOWN_J + 1))
                for b in range(2):
                    first = PIECES + 3 + b * DOWN_J
                    if n in range(first, first + DOWN_J):
                        down.load_v(sp, b, b, n - first)
                    first += 2 * DOWN_J
                    if n in range(first, first + DOWN_J):
                        down.load_weights(sp, b, b, n - first)
            for n in range(2):
                sp.wait_ge(a_stored[n], 16 * (PEER_K // 2 + 1))

        @block.gpsimd
        def _(pool):
            def low_part(j, n):
                pool.wait_ge(high, j + 1)
                pool.tensor_tensor(ul[:, n, :, :], u[:, n, :, :], bits32(uh[:, n, :, :]), ALU.subtract).then_inc(low, 1)

            for n in range(2):
                low_part(n, n)
            for tt in range(TT):
                with pool.Fori(0, ALONE // 2) as i:
                    for n in range(2):
                        low_part(i * 2 + (tt * NJ + n + 2), n)
                with pool.Fori(0, WITH // 2) as i:
                    for n in range(2):
                        for b in range(FOURS):
                            hold(pool, m, second_low, i * (2 * FOURS) + (tt * (P // 4) + n * FOURS + b + 1))
                            t = bass.ds(i * (2 * STEP) + (n * STEP + 4 * b), 4)
                            o = hot_h[:, 4 * b:4 * b + 4, :]
                            pool.tensor_tensor(o, bits32(o), bits32(gate_h[:, t]).unsqueeze(2).broadcast_to([P, 4, P]),
                                               ALU.mult).then_inc(second_high, 1)
                        low_part(i * 2 + (tt * NJ + ALONE + n + 2), n)
            with pool.Fori(0, TAIL // 2 - 1) as i:
                for n in range(2):
                    low_part(i * 2 + (PEER_K - TAIL + n + 2), n)

        @block.vector
        def _(dve):
            st = Steps(dve, dve_s)

            def top16(values, rest, v, i):
                st.done(dve.max(v[:, 0:8], values))
                dve.max_index(i[:, 0:8], v[:, 0:8], values)
                st.done(dve.match_replace(rest, v[:, 0:8], values, NEG))
                st.done(dve.max(v[:, 8:16], rest))
                return dve.max_index(i[:, 8:16], v[:, 8:16], rest)

            flat = lambda x: x.rearrange("p h k -> p (h k)")
            grid = lambda x: x.rearrange("p (h k a) -> p h k a", h=PEER_H, k=TOPK)
            iota = sq(m, "iota")
            iotas = iota.unsqueeze(1).broadcast_to([P, 4, P])
            for tt in range(TT):
                scores = m.scores[:, tt, :, :]
                cand = flat(scores)
                for hz in range(NHZ):
                    last = top16(scores[:, hz, :], spare[:, hz * PEER_K:(hz + 1) * PEER_K], top_v[:, hz, :], top_i[:, hz, :])
                st.done(last)
                dve.tensor_copy(top_f[:, :, :], top_i[:, :, :])
                tv = top_v[:, :, :].rearrange("p (h z) k -> p h z k", z=2)
                st.done(dve.tensor_tensor(grid(cand), tv[:, :, 0, :].unsqueeze(3).broadcast_to([P, PEER_H, TOPK, TOPK]),
                                          tv[:, :, 1, :].unsqueeze(2).broadcast_to([P, PEER_H, TOPK, TOPK]), ALU.add))
                for h in range(PEER_H):
                    c, rest = (x[:, h * TOPK * TOPK:(h + 1) * TOPK * TOPK] for x in (cand, spare))
                    last = top16(c, rest, best[:, h, :], pos[:, h, :])
                st.done(last)
                top1 = best[:, :, 0:1].broadcast_to([P, PEER_H, TOPK])
                gate = chosen[:, 2, :].rearrange("p (h k) -> p h k", k=TOPK)
                dve.tensor_tensor(gate, best[:, :, :], top1, ALU.subtract).then_inc(maxed, 1)
                for z in range(2):
                    if z == 0:
                        st.done(dve.tensor_scalar(part[:, :], flat(pos[:, :, :]), 4, None, ALU.logical_shift_right))
                    else:
                        st.done(dve.tensor_scalar(part[:, :], flat(pos[:, :, :]), 15, None, ALU.bitwise_and))
                    st.done(dve.tensor_copy(part_f[:, :], part[:, :]))
                    eq = spare[:, :].rearrange("p (n a) -> p n a", a=TOPK)
                    st.done(dve.tensor_tensor(eq, part_f[:, :].unsqueeze(2).broadcast_to([P, HK, TOPK]),
                                              iota[:, 0:TOPK].unsqueeze(1).broadcast_to([P, HK, TOPK]), ALU.is_equal))
                    tf = top_f[:, :, :].rearrange("p (h z) k -> p h z k", z=2)[:, :, z, :].unsqueeze(2)
                    st.done(dve.tensor_tensor(grid(spare[:, :]), grid(spare[:, :]), tf.broadcast_to([P, PEER_H, TOPK, TOPK]), ALU.mult))
                    st.done(dve.tensor_reduce(chosen[:, z, :], eq, AX.X, ALU.add))
                dve.wait_ge(exped, tt + 1)
                st.done(dve.tensor_reduce(sums[:, :], gate, AX.X, ALU.add))
                st.done(dve.reciprocal(sums[:, :], sums[:, :]))
                dve.tensor_tensor(gate, gate, sums[:, :].unsqueeze(2).broadcast_to([P, PEER_H, TOPK]), ALU.mult).then_inc(made, 1)
                dve.wait_ge(t_copied, tt + 1)
                st.done(dve.tensor_tensor(gate_l[:, :], high_t[:, 2, :], bits32(gate_h[:, :]), ALU.subtract))
                with dve.Fori(0, WITH) as i:
                    for b in range(FOURS):
                        k = i * FOURS + (tt * (P // 4) + b + 1)
                        four, t = slice(4 * b, 4 * b + 4), bass.ds(i * STEP + 4 * b, 4)
                        spread_over = lambda x: x.unsqueeze(2).broadcast_to([P, 4, P])
                        dve.wait_ge(spread, k)
                        dve.tensor_tensor(hot_h[:, four, :], iotas, spread_over(high_t[:, 1, t]), ALU.is_equal).then_inc(second_eq, 1)
                        dve.tensor_tensor(hot_i[:, four, :], iotas, spread_over(high_t[:, 0, t]), ALU.is_equal)
                        dve.wait_ge(second_eq, k)
                        dve.tensor_tensor(hot_l[:, four, :], bits32(hot_h[:, four, :]), spread_over(gate_l[:, t]), ALU.mult).then_inc(second_low, 1)

        @block.scalar
        def _(act):
            act.sem_inc(gs_done, FOURS)
            act.sem_inc(gelu, 2)

            def split(j, n):
                act.wait_ge(u_in[n], j * 8 + (16 - 8 * n))
                act.activation(uh[:, n, :, :], u[:, n, :, :], ACT.Copy).then_inc(high, 1)

            def key(j, n, more=True):
                act.wait_ge(prod, j + 1)
                act.wait_ge(a_stored[n], j * 8 + (16 - 8 * n))
                act.activation(av[:, n, :], m.ps[:, n, :], ACT.Gelu).then_inc(gelu, 1)
                if more:
                    split(j + 2, n)

            for n in range(2):
                split(n, n)
            for tt in range(TT):
                gate = chosen[:, 2, :]
                with act.Fori(0, ALONE // 2) as i:
                    for n in range(2):
                        key(i * 2 + (tt * NJ + n), n)
                act.wait_ge(maxed, tt + 1)
                act.activation(gate, gate, ACT.Exp).then_inc(exped, 1)
                act.wait_ge(turned, tt + 1)
                act.activation(high_t[:, :, :], m.ps[:, 6, 0:3 * P].rearrange("p (a n) -> p a n", a=3), ACT.Copy)
                act.activation(gate_h[:, :], m.ps[:, 6, 2 * P:3 * P], ACT.Copy).then_inc(t_copied, 1)

                if tt:
                    act.wait_ge(stored, 16 * PIECES * tt)
                with act.Fori(0, WITH // 2) as i:
                    for n in range(2):
                        key(i * 2 + (tt * NJ + ALONE + n), n)
                        for b in range(FOURS):
                            k = tt * (P // 4) + n * FOURS + b
                            hold(act, m, spread, i * (2 * FOURS) + (k + 1 + FOURS))
                            dst = gs[:, :, bass.ds(i * (2 * STEP) + (n * STEP + 4 * b), 4)].rearrange("p j t -> p t j")
                            act.activation(dst, m.ps[:, 2 + b, :].rearrange("p (t j) -> p t j", t=4), ACT.Copy).then_inc(gs_done, 1)
            with act.Fori(0, TAIL // 2 - 1) as i:
                for n in range(2):
                    key(i * 2 + (PEER_K - TAIL + n), n)
            for n in range(2):
                key(PEER_K - 2 + n, n, False)

        @block.tensor
        def _(pe):
            pe.sem_inc(spread, FOURS)

            def key(j, n):
                pe.wait_ge(low, j + 1)
                pe.wait_ge(gelu, j + 1)
                products(pe, m.ps[:, n, :], [(uh[:, n, k, :], ul[:, n, k, :]) for k in range(KT)],
                         [(m.nh[:, k, :], m.nl[:, k, :]) for k in range(KT)]).then_inc(prod, 1)

            for tt in range(TT):
                with pe.Fori(0, ALONE // 2) as i:
                    for n in range(2):
                        key(i * 2 + (tt * NJ + n), n)
                pe.wait_ge(made, tt + 1)
                for n in range(3):
                    last = pe.transpose(m.ps[:, 6, n * P:(n + 1) * P], chosen[:, n, :], sq(m, "eye"))
                last.then_inc(turned, 1)
                with pe.Fori(0, WITH // 2) as i:
                    for n in range(2):
                        key(i * 2 + (tt * NJ + ALONE + n), n)
                        for b in range(FOURS):
                            k = tt * (P // 4) + n * FOURS + b
                            pe.wait_ge(second_low, i * (2 * FOURS) + (k + 1))
                            pe.wait_ge(second_high, i * (2 * FOURS) + (k + 1))
                            pe.wait_ge(gs_done, i * (2 * FOURS) + (k + 1))
                            for q in range(4 * b, 4 * b + 4):
                                o = m.ps[:, 2 + b, (q % 4) * P:(q % 4 + 1) * P]
                                pe.matmul(o, hot_i[:, q, :], hot_h[:, q, :], start=True, stop=False)
                                last = pe.matmul(o, hot_i[:, q, :], hot_l[:, q, :], start=False, stop=True)
                            last.then_inc(spread, 1)
            with pe.Fori(0, TAIL // 2) as i:
                for n in range(2):
                    key(i * 2 + (PEER_K - TAIL + n), n)


class DownLoads:

    def __init__(self, nc, m, g_dense, a_dense):
        r = m.region(AT_END - KB_GATES, AT_END)
        self.v = r.take("down_v", [P, 2, DOWN_J, D])
        self.a, self.g = (r.take(f"down_{x}", [P, 2, DOWN_J, T]) for x in ("gelu", "gates"))
        self.v_in, self.a_in, self.g_in = ([nc.alloc_semaphore(name=f"down_{x}{b}_loaded") for b in range(2)] for x in "vag")
        self.ev = m.ins["expert_v"].rearrange("p (j n) -> p j n", n=D)
        self.ad, self.gd = (x.rearrange("j i t -> i j t") for x in (a_dense, g_dense))

    def load_v(self, sp, n, b, j):
        sp.dma_start(self.v[:, b, j:j + 1, :], self.ev[:, bass.ds(n * DOWN_J + j, 1), :]).then_inc(self.v_in[b], 16)

    def load_weights(self, sp, n, b, j):
        sp.dma_start(self.a[:, b, j:j + 1, :], self.ad[:, bass.ds(n * DOWN_J + j, 1), :]).then_inc(self.a_in[b], 16)
        sp.dma_start(self.g[:, b, j:j + 1, :], self.gd[:, bass.ds(n * DOWN_J + j, 1), :]).then_inc(self.g_in[b], 16)


def down_stage(nc, m, down):
    JB = DOWN_J
    NB = PEER_K // JB
    r = m.region(AT_XT, AT_END - KB_GATES)
    take = lambda name, shape, dt=F32: r.take(f"down_{name}", shape, dt)
    v, a, g, v_in, a_in, g_in = down.v, down.a, down.g, down.v_in, down.a_in, down.g_in
    vh, vl = ([take(f"v{b}_{x}", [P, JB, D], F32R) for b in range(2)] for x in ("high", "low"))
    wh, wl = take("w_high", [P, 2, JB, T], F32R), take("w_low", [P, 2, JB, T], F32R)
    m.sems += v_in + a_in + g_in
    sem = lambda name: m.sem(f"down_{name}")
    prod, weighed, w_high, w_low, v_high, v_low, added = (sem(x) for x in ("products", "weighed", "w_high_done", "w_low_done",
                                                                           "v_high_done", "v_low_done", "added"))
    with nc.Block() as block:

        @block.sync
        def _(sp):
            with sp.Fori(1, NB // 2) as i:
                for b in range(2):
                    sp.wait_ge(w_low, i * (2 * JB) + (b - 1) * JB)
                    for j in range(JB):
                        down.load_weights(sp, i * 2 + b, b, j)
                    sp.wait_ge(v_low, i * (2 * JB) + (b - 1) * JB)
                    for j in range(JB):
                        down.load_v(sp, i * 2 + b, b, j)

        @block.scalar
        def _(act):
            with act.Fori(0, NB // 2) as i:
                for b in range(2):
                    act.wait_ge(v_in[b], i * (16 * JB) + 16 * JB)
                    act.wait_ge(prod, i * 16 + (8 * b + 8))
                    for j in range(JB):
                        act.activation(vh[b][:, j, :], v[:, b, j, :], ACT.Copy).then_inc(v_high, 1)
                        act.wait_ge(weighed, i * (2 * JB) + (b * JB + j + 1))
                        act.activation(wh[:, b, j, :], a[:, b, j, :], ACT.Copy).then_inc(w_high, 1)

        @block.gpsimd
        def _(pool):
            with pool.Fori(0, NB // 2) as i:
                for b in range(2):
                    for j in range(JB):
                        pool.wait_ge(v_high, i * (2 * JB) + (b * JB + j + 1))
                        pool.tensor_tensor(vl[b][:, j, :], v[:, b, j, :], bits32(vh[b][:, j, :]), ALU.subtract).then_inc(v_low, 1)

        @block.vector
        def _(dve):
            def weigh(n, b):
                for j in range(JB):
                    k = n * JB + (j + 1)
                    if j == 0:
                        use = (n * 8 + (16 - 8 * b)) * JB
                        dve.wait_ge(a_in[b], use)
                        dve.wait_ge(g_in[b], use)
                    dve.tensor_tensor(a[:, b, j, :], a[:, b, j, :], g[:, b, j, :], ALU.mult).then_inc(weighed, 1)
                for j in range(JB):
                    dve.wait_ge(w_high, n * JB + (j + 1))
                    dve.tensor_tensor(wl[:, b, j, :], a[:, b, j, :], bits32(wh[:, b, j, :]), ALU.subtract).then_inc(w_low, 1)

            def add(n):
                for q in range(8):
                    half, tt = divmod(q, 4)
                    dve.wait_ge(prod, n * 8 + (16 + q + 1))
                    o = m.h[:, tt, half * CW:(half + 1) * CW]
                    dve.tensor_tensor(o, o, m.ps[:, q, :], ALU.add).then_inc(added, 1)

            dve.sem_inc(added, 8)
            weigh(0, 0)
            with dve.Fori(0, NB // 2 - 1) as i:
                weigh(i * 2 + 1, 1)
                add(i * 2)
                weigh(i * 2 + 2, 0)
                add(i * 2 + 1)
            weigh(NB - 1, 1)
            add(NB - 2)
            add(NB - 1)

        @block.tensor
        def _(pe):
            pe.sem_inc(prod, 16)
            with pe.Fori(0, NB // 2) as i:
                for b in range(2):
                    pe.wait_ge(v_low, i * (2 * JB) + (b + 1) * JB)
                    pe.wait_ge(w_low, i * (2 * JB) + (b + 1) * JB)
                    for q in range(8):
                        half, tt = divmod(q, 4)
                        t, c = slice(tt * P, (tt + 1) * P), slice(half * CW, (half + 1) * CW)
                        pe.wait_ge(added, i * 16 + (8 * b + q + 1))
                        products(pe, m.ps[:, q, :], [(wh[:, b, j, t], wl[:, b, j, t]) for j in range(JB)],
                                 [(vh[b][:, j, c], vl[b][:, j, c]) for j in range(JB)]).then_inc(prod, 1)


def output_stage(nc, m, last_stage):
    KP = PLE // P
    r = m.region(AT_XT, AT_END)
    norm = NormT(nc, m, r, "ple_norm", COL_PLE)
    pT = r.take("p_t", [P, KP, T])
    wp = r.take("w_ple_proj", [P, 2, KP, CW])
    gain = r.take("final_gain", [P, D])
    sg = r.take("ple_gate", [P, 4, CW])
    fin = r.take("final_stat", [P, 3, TT])
    y = norm.xs
    (g_out, gate, added, squared, meaned, rooted, dve_s, y_done, p_in, stored) = (
        m.sem(f"ple_{x}") for x in ("projected", "gate", "added", "squared", "meaned", "rooted", "dve_steps",
                                    "y_done", "p_loaded", "stored"))
    stream = Stream(m, r, r, "ple", [m.ins["w_ple_gate"][n] for n in range(2)])
    with nc.Block() as block:

        @block.sync
        def _(sp):
            sp.dma_start(pT[:, :, :], m.ins["p_t"].rearrange("p (k t) -> p k t", t=T)).then_inc(p_in, 16)
            sp.dma_start(wp[:, :, :, :].rearrange("p n k c -> p n (k c)"), m.ins["w_ple_proj"].rearrange("n p c -> p n c")).then_inc(p_in, 16)
            sp.dma_start(gain[:, :], m.ins["norm_final"].broadcast_to([P, D])).then_inc(p_in, 16)
            stream.sp(sp)
            for tt in range(TT):
                sp.wait_ge(y_done, tt + 1)
                sp.dma_start(m.outs[tt // TS][0, (tt % TS) * P:(tt % TS + 1) * P, :], y[:, tt, :]).then_inc(stored, 16)
            sp.wait_ge(stored, 16 * TT)

        @block.gpsimd
        def _(pool):
            stream.pool(pool)

        @block.tensor
        def _(pe):
            norm.pe(pe)
            pe.wait_ge(norm.out_done, KT)
            pe.wait_ge(p_in, 48)
            for n in range(2):
                for tt in range(TT):
                    if n:
                        pe.wait_ge(added, tt + 1)
                    for k in range(KP):
                        last = pe.matmul(m.ps[:, 4 + tt, :], pT[:, k, tt * P:(tt + 1) * P], wp[:, n, k, :], start=k == 0, stop=k == KP - 1)
                    last.then_inc(g_out, 1)
                stream.pe(pe, n, 0, lambda tt: None, (m.nh, m.nl), True)

        @block.scalar
        def _(act):
            stream.high(act, 0)
            stream.high(act, 1)
            norm.act(act)

            def gates(n):
                for tt in range(TT):
                    g = 4 * n + tt
                    act.wait_ge(stream.prod, g + 1)
                    if g >= 4:
                        act.wait_ge(added, g - 3)
                    act.activation(sg[:, g % 4, :], m.ps[:, g % 4, :], ACT.Sigmoid).then_inc(gate, 1)

            for n in range(2):
                stream.act(act, n, lambda: gates(n))
            for tt in range(TT):
                act.wait_ge(added, 4 + tt + 1)
                act.activation(y[:, tt, :], m.h[:, tt, :], ACT.Square, accum_out=fin[:, 0, tt:tt + 1]).then_inc(squared, 1)
            act.wait_ge(meaned, 1)
            act.activation(fin[:, 2, :], fin[:, 1, :], ACT.Sqrt).then_inc(rooted, 1)

        @block.vector
        def _(dve):
            norm.dve(dve)
            st = Steps(dve, dve_s)
            for g in range(8):
                n, tt = divmod(g, 4)
                dve.wait_ge(gate, g + 1)
                dve.wait_ge(g_out, g + 1)
                st.done(dve.tensor_tensor(sg[:, tt, :], m.ps[:, 4 + tt, :], sg[:, tt, :], ALU.mult))
                o = m.h[:, tt, n * CW:(n + 1) * CW]
                dve.tensor_tensor(o, o, sg[:, tt, :], ALU.add).then_inc(added, 1)
            dve.wait_ge(squared, TT)
            dve.tensor_scalar(fin[:, 1, :], fin[:, 0, :], 1.0 / D, EPS, ALU.mult, ALU.add).then_inc(meaned, 1)
            dve.wait_ge(rooted, 1)
            dve.wait_ge(p_in, 48)
            st.done(dve.reciprocal(fin[:, 0, :], fin[:, 2, :]))
            for tt in range(TT):
                dve.scalar_tensor_tensor(y[:, tt, :], m.h[:, tt, :], fin[:, 0, tt:tt + 1], gain[:, :],
                                         ALU.mult, ALU.mult).then_inc(y_done, 1)


def layouts(**a):
    f = {k: np.asarray(v) for k, v in a.items()}
    chunk = lambda w: np.ascontiguousarray(w.reshape(w.shape[0] // P, P, w.shape[1] // CW, CW).transpose(2, 1, 0, 3)
                                           .reshape(w.shape[1] // CW, P, -1))
    cols = lambda v: v.reshape(-1, P).T
    w = f["w_in"][0]
    at = np.cumsum([0, 1024, 2048, 32, 3072, 1024, 16, 16, 1024, 1024])
    part = lambda n: w[:, at[n]:at[n + 1]]
    conv_w = np.concatenate([part(1), part(3)], axis=1)
    gates = np.concatenate([part(0), part(7), part(4), part(8)], axis=1)
    small = np.concatenate([part(2), part(5), part(6)], axis=1)
    taps = np.concatenate([f["ssd_conv_w"][0], f["gdn_conv_w"][0]], axis=1)
    bias = np.concatenate([f["ssd_conv_b"][0], np.zeros(3 * GDN_H * GDN_D, np.float32)])
    conv = np.concatenate([taps, bias[None]], axis=0).reshape(5, N_CONV, P).transpose(2, 1, 0).reshape(P, -1)
    colp = np.concatenate([conv, cols(f["norm_mix"][0]), cols(f["norm_ffn"][0]), cols(f["norm_ple"][0]),
                           cols(f["ssd_norm"][0]), cols(f["gdn_norm"][0])], axis=1)
    rowp = np.concatenate([f["ssd_dt_bias"][0].ravel(), f["gdn_dt_bias"][0].ravel(), f["ssd_a_log"][0].ravel(),
                           f["gdn_a_log"][0].ravel(), f["ssd_d"][0]])[None]
    eu = f["expert_u"][0].reshape(P, PEER_K, KT, P)
    ev = f["expert_v"][0].reshape(P, PEER_K * D)
    keys = f["peer_keys"][0].reshape(NHZ, PEER_K, P).transpose(2, 0, 1).reshape(P, NHZ * PEER_K)
    d = {
        "x_prompt": f["x_prompt"], "x_sample": f["x_sample"],
        "p_t": np.concatenate([f["p_prompt"][0, 0], f["p_sample"][0, 0]], axis=0).T.reshape(PLE // P, P, T).transpose(1, 0, 2)
        .reshape(P, -1),
        "squares": squares(), "norm_final": f["norm_final"][None], "column_params": colp, "row_params": rowp,
        "w_conv": np.ascontiguousarray(conv_w.reshape(KT, P, -1, 2 * P).transpose(2, 1, 0, 3)).reshape(-1, P, KT * 2 * P),
        "w_gates": chunk(gates),
        "w_small": small.reshape(KT, P, 64).transpose(1, 0, 2).reshape(P, -1),
        "w_ssd_out": chunk(f["w_ssd_out"][0]), "w_gdn_out": chunk(f["w_gdn_out"][0]), "w_out": chunk(f["w_out"][0]),
        "peer_query": chunk(f["peer_query"][0]), "w_ple_gate": chunk(f["w_ple_gate"][0]),
        "w_ple_proj": chunk(f["w_ple_proj"][0]),
        "peer_keys": keys,
        "expert_u": eu.transpose(1, 3, 2, 0).reshape(PEER_K, P, D),
        "expert_v": ev,
    }
    return {k: np.ascontiguousarray(v) for k, v in d.items()}


def program(nc, arrays, last_stage=99):
    ins = {k: nc.dram_tensor(k, a.shape, F32, kind="ExternalInput").ap() for k, a in arrays.items()}
    outs = [nc.dram_tensor(n, (1, L, D), F32, kind="ExternalOutput").ap() for n in ("y_prompt", "y_sample")]
    build(nc, ins, outs, last_stage)


def kernel(**inputs):
    import concourse.bacc as bacc
    from concourse.bass_utils import run_bass_kernel_spmd

    arrays = layouts(**inputs)
    nc = bacc.Bacc("TRN2", target_bir_lowering=False, num_devices=1, dynamic_dma_scratch_size=1024)
    program(nc, arrays)
    r = run_bass_kernel_spmd(nc, [arrays], core_ids=[0])
    return r.results[0]["y_prompt"], r.results[0]["y_sample"]
```

```python
import numpy as np

import concourse.bass as bass
from concourse import mybir
from concourse.alu_op_type import AluOpType as ALU

ACT = mybir.ActivationFunctionType
AX = mybir.AxisListType
F32 = mybir.dt.float32
F32R = mybir.dt.float32r
U32 = mybir.dt.uint32

P = 128
SEQS = 2
L = 256
T = SEQS * L
TT = T // P
TS = L // P
D = 1024
KT = D // P
PLE = 256
EPS = 1e-6
SSD_H, SSD_P, SSD_G, SSD_N = 16, 64, 4, 128
SSD_R = SSD_H // SSD_G
GDN_H, GDN_D = 8, 128
PEER_H, PEER_K, TOPK = 8, 128, 16
NHZ = 2 * PEER_H
HK = PEER_H * TOPK
CW = 512
N_CONV = (SSD_H * SSD_P + 2 * SSD_G * SSD_N + 3 * GDN_H * GDN_D) // P
NEG = -3.0e38

SQUARES = ["eye", "ones", "le", "ge", "lt", "gt"] + [f"lvl{b}" for b in (1, 2, 4, 8, 16, 32, 64)] + ["iota"]
LEVELS = (2, 4, 8, 16, 32, 64)

COL_CONV = 0
COL_MIX = COL_CONV + 5 * N_CONV
COL_FFN = COL_MIX + KT
COL_PLE = COL_FFN + KT
COL_SSDN = COL_PLE + KT
COL_GDNN = COL_SSDN + KT
COLS = COL_GDNN + 1

ROW_BIAS = 0
ROW_ALOG = 48
ROW_D = 96
ROWS = 112


def squares():
    p, c = np.arange(P)[:, None], np.arange(P)[None, :]
    m = {"eye": p == c, "ones": p == p + 0 * c, "le": p <= c, "ge": p >= c, "lt": p < c, "gt": p > c, "iota": c + 0 * p}
    for b in (1, 2, 4, 8, 16, 32, 64):
        m[f"lvl{b}"] = (p // (2 * b) == c // (2 * b)) & (p // b != c // b)
    return np.concatenate([np.broadcast_to(m[k], (P, P)).astype(np.float32) for k in SQUARES], axis=1)


def halves():
    p, c = np.arange(P)[:, None], np.arange(P)[None, :]
    return np.concatenate([np.where(p // b % 2 == 0, p >= c, p <= c).astype(np.float32) for b in LEVELS], axis=1)


class Steps:

    def __init__(self, eng, sem):
        self.eng, self.sem, self.base, self.k, self.i, self.per = eng, sem, 0, 0, None, 0

    def loop(self, i, per):
        self.i, self.per, self.base, self.k = i, per, self.base + self.k, 0

    def end(self, trips):
        assert self.k == self.per, (self.k, self.per)
        self.base, self.k, self.i = self.base + trips * self.per, 0, None

    def value(self):
        return self.base + self.k if self.i is None else self.i * self.per + (self.base + self.k)

    def done(self, ins):
        self.k += 1
        ins.then_inc(self.sem, 1)
        self.eng.wait_ge(self.sem, self.value())


def hold(eng, m, sem, value):
    eng.wait_ge(sem, value)
    eng.sem_inc(m.held[eng.engine], 1)


class Region:

    def __init__(self, nc, start, end):
        self.nc, self.at, self.end = nc, start, end

    def take(self, name, shape, dt=F32):
        size = 4 * int(np.prod(shape[1:]))
        size += -size % 32
        assert self.at + size <= self.end, (name, self.at + size - self.end)
        t = self.nc.alloc_sbuf_tensor_at(f"{name}_sb", shape, dt, offset=self.at)
        self.at += size
        return t


def bits32(x):
    return x.bitcast(F32)


class M:
    pass


KB = 1024
AT_XT, AT_OG, AT_CH, AT_WORK, AT_END = 57.25, 73.25, 89.25, 169.25, 222.5
AT_SCORES = 57.25
KB_GATES = 64
DOWN_J = 4


def build(nc, ins, outs):
    m = M()
    m.ins, m.outs, m.sems = ins, outs, []
    base = nc.sbuf_base + -nc.sbuf_base % 64

    def sem(name):
        m.sems.append(nc.alloc_semaphore(name=name))
        return m.sems[-1]

    def region(start, end):
        return Region(nc, base + int(start * KB), base + int(end * KB))

    m.sem, m.region = sem, region
    m.held = {e.engine: nc.alloc_semaphore(name=n) for e, n in ((nc.scalar, "act_passed_a_wait"), (nc.gpsimd, "pool_passed_a_wait"))}
    r = region(0, AT_XT)
    m.sq = r.take("squares", [P, len(SQUARES), P])
    m.colp = r.take("column_params", [P, COLS])
    m.rowp = r.take("row_params", [P, ROWS])
    m.h = r.take("h", [P, TT, D])
    m.nh = r.take("n_high", [P, KT, T], F32R)
    m.nl = r.take("n_low", [P, KT, T], F32R)
    m.stat = r.take("stat", [P, 3, TT])
    m.eps = r.take("eps", [P, 1])
    m.ps = nc.alloc_psum_tensor("ps", [P, 8, CW], F32)
    mixer_stages(nc, m)
    expert_stages(nc, m)
    output_stage(nc, m)
    end_stage(nc, m)


def products(pe, out, stationary, moving, ready=lambda k: None):
    n = len(stationary)
    for k, ((ah, al), (bh, bl)) in enumerate(zip(stationary, moving)):
        ready(k)
        pe.matmul(out, ah, bh, start=k == 0, stop=False)
        pe.matmul(out, ah, bl, start=False, stop=False)
        last = pe.matmul(out, al, bh, start=False, stop=k == n - 1)
    return last


def sq(m, name):
    return m.sq[:, SQUARES.index(name), :]


def sq_pair(m, name, mid):
    n = SQUARES.index(name)
    return m.sq[:, n:n + 2, :].unsqueeze(2).broadcast_to([P, 2, mid, P])


def end_stage(nc, m):
    nc.clear_and_free_semaphores(m.sems)
    m.sems = []
    nc.all_engine_barrier()


class NormT:

    def __init__(self, nc, m, region, tag, col):
        self.nc, self.m, self.col = nc, m, col
        self.xs = region.take(f"{tag}_scaled", [P, TT, D])
        (self.sq_done, self.ms_done, self.root_done, self.vec, self.scaled, self.turned, self.high_done, self.out_done) = (
            m.sem(f"{tag}_{x}") for x in ("squares_done", "mean_done", "root_done", "vector_steps", "scaled_done", "turned",
                                          "high_done", "low_done"))

    def act(self, act, ready=lambda tt: None, between=lambda: None):
        m = self.m
        for tt in range(TT):
            ready(tt)
            act.activation(self.xs[:, tt, :], m.h[:, tt, :], ACT.Square,
                           accum_out=m.stat[:, 0, tt:tt + 1]).then_inc(self.sq_done, 1)
        act.wait_ge(self.ms_done, 1)
        act.activation(m.stat[:, 2, :], m.stat[:, 1, :], ACT.Sqrt).then_inc(self.root_done, 1)
        between()
        for kt in range(KT):
            act.wait_ge(self.turned, kt + 1)
            act.activation(m.nh[:, kt, :], m.ps[:, kt, :], ACT.Copy,
                           scale=m.colp[:, self.col + kt:self.col + kt + 1]).then_inc(self.high_done, 1)

    def dve(self, dve):
        m, st = self.m, Steps(dve, self.vec)
        dve.wait_ge(self.sq_done, TT)
        dve.tensor_scalar(m.stat[:, 1, :], m.stat[:, 0, :], 1.0 / D, EPS, ALU.mult, ALU.add).then_inc(self.ms_done, 1)
        dve.wait_ge(self.root_done, 1)
        st.done(dve.reciprocal(m.stat[:, 0, :], m.stat[:, 2, :]))
        for tt in range(TT):
            dve.tensor_scalar(self.xs[:, tt, :], m.h[:, tt, :], m.stat[:, 0, tt:tt + 1], None,
                              ALU.mult).then_inc(self.scaled, 1)
        for kt in range(KT):
            dve.wait_ge(self.high_done, kt + 1)
            dve.scalar_tensor_tensor(m.nl[:, kt, :], m.ps[:, kt, :], m.colp[:, self.col + kt:self.col + kt + 1],
                                     bits32(m.nh[:, kt, :]), ALU.mult, ALU.subtract).then_inc(self.out_done, 1)

    def pe(self, pe):
        m = self.m
        for tt in range(TT):
            pe.wait_ge(self.scaled, tt + 1)
            for kt in range(KT):
                last = pe.transpose(m.ps[:, kt, tt * P:(tt + 1) * P], self.xs[:, tt, kt * P:(kt + 1) * P], sq(m, "eye"))
                if tt == TT - 1:
                    last.then_inc(self.turned, 1)


def mixer_stages(nc, m):
    m.xt = m.region(AT_XT, AT_OG).take("ssd_tokens", [P, TT, D])
    m.og = m.region(AT_OG, AT_CH).take("gdn_tokens", [P, TT, D])
    m.ch = m.region(AT_CH, AT_WORK).take("channels", [P, N_CONV, T])
    r = m.region(AT_END - 4.25, AT_END)
    m.small = r.take("small", [P, TT, 64])
    m.decay = r.take("decay", [P, TT, 48])
    m.edk = r.take("gdn_decays", [P, 4, TT, 16])
    m.ned = r.take("gdn_neg_decay", [P, 2, TT, 16])
    for stage in (project_stage, turn_stage, ssd_stage, gdn_stage, merge_stage):
        stage(nc, m)
        end_stage(nc, m)


def log1p_coeffs():
    return [1.0 / (2 * n + 1) for n in range(0, 10)]


def project_stage(nc, m):
    norm = NormT(nc, m, m.region(AT_CH, AT_WORK), "mix_norm", COL_MIX)
    const_in, x_in = m.sem("constants_loaded"), [m.sem(f"tokens{tt}_loaded") for tt in range(TT)]
    CC = 2 * P
    CHUNKS = 4
    TILES = CHUNKS * 2
    TRIPS = N_CONV // TILES
    raw_r, split_r = m.region(AT_XT, AT_CH), m.region(AT_WORK, AT_END - 4.25)
    w = raw_r.take("w_slots", [P, 2, KT, CC])
    tmp = raw_r.take("small_tmp", [P, 5, TT, 48])
    ws = raw_r.take("w_small", [P, KT, 64])
    wsh, wsl = raw_r.take("w_small_high", [P, KT, 64], F32R), raw_r.take("w_small_low", [P, KT, 64], F32R)
    tab = raw_r.take("a_coefficients", [P, 48])
    small_t = raw_r.take("small_t", [64, T])
    wh, wl = split_r.take("w_high", [P, 2, KT, CC], F32R), split_r.take("w_low", [P, 2, KT, CC], F32R)
    w_in = [m.sem(f"w_slot{j}_loaded") for j in range(2)]
    ws_in, small_high, small_low = m.sem("w_small_loaded"), m.sem("w_small_high"), m.sem("w_small_low")
    high, low = m.sem("w_high_done"), m.sem("w_low_done")
    prod, taps0, conv = m.sem("channels_product"), m.sem("centre_tap"), m.sem("other_taps")
    act_s, dve_s, act_small, dve_small = (m.sem(x) for x in ("conv_act_steps", "conv_dve_steps", "small_act", "small_dve"))
    small_prod, small_out, gate_out = m.sem("small_product"), m.sem("small_copied"), m.sem("gdn_decay_products")
    small_staged, small_turned = m.sem("small_staged"), m.sem("small_turned")
    par = m.colp[:, COL_CONV:COL_MIX].rearrange("p (c k) -> p c k", k=5)

    def tap(c, k):
        return par[:, bass.ds(c, 1), k:k + 1].rearrange("p a b -> p (a b)")

    with nc.Block() as block:

        @block.sync
        def _(sp):
            for tt in range(TT):
                x = m.ins["x_prompt"] if tt < TS else m.ins["x_sample"]
                sp.dma_start(m.h[:, tt, :], x[0, (tt % TS) * P:(tt % TS + 1) * P, :]).then_inc(x_in[tt], 16)
            sp.dma_start(m.sq[:, :, :], m.ins["squares"].rearrange("p (n c) -> p n c", c=P)).then_inc(const_in, 16)
            sp.dma_start(m.colp[:, :], m.ins["column_params"]).then_inc(const_in, 16)
            sp.dma_start(m.rowp[:, :], m.ins["row_params"].broadcast_to([P, ROWS])).then_inc(const_in, 16)
            sp.dma_start(ws[:, :, :], m.ins["w_small"].rearrange("p (k n) -> p k n", n=64)).then_inc(ws_in, 16)

            def load(i, c):
                src = m.ins["w_conv"][bass.ds(i * CHUNKS + c, 1)].rearrange("a p (k n) -> p (a k) n", n=CC)
                sp.dma_start(w[:, c % 2, :, :], src).then_inc(w_in[c % 2], 16)

            for c in range(2):
                load(0, c)
            for c in range(2, CHUNKS):
                sp.wait_ge(low, c - 1)
                load(0, c)
            with sp.Fori(1, TRIPS) as i:
                for c in range(CHUNKS):
                    sp.wait_ge(low, i * CHUNKS + (c - 1))
                    load(i, c)

        @block.gpsimd
        def _(pool):
            pool.memset(m.eps[:, :], EPS)
            pool.wait_ge(small_high, 1)
            pool.tensor_tensor(wsl[:, :, :], ws[:, :, :], bits32(wsh[:, :, :]), ALU.subtract).then_inc(small_low, 1)
            with pool.Fori(0, TRIPS) as i:
                for c in range(CHUNKS):
                    pool.wait_ge(high, i * CHUNKS + (c + 1))
                    pool.tensor_tensor(wl[:, c % 2, :, :], w[:, c % 2, :, :], bits32(wh[:, c % 2, :, :]),
                                       ALU.subtract).then_inc(low, 1)

        @block.tensor
        def _(pe):
            pe.wait_ge(const_in, 48)
            norm.pe(pe)
            pe.wait_ge(small_low, 1)
            products(pe, m.ps[0:64, 0, :], [(wsh[:, k, :], wsl[:, k, :]) for k in range(KT)],
                     [(m.nh[:, k, :], m.nl[:, k, :]) for k in range(KT)],
                     lambda k: pe.wait_ge(norm.out_done, k + 1)).then_inc(small_prod, 1)
            pe.wait_ge(small_staged, 1)
            for tt in range(TT):
                last = pe.transpose(m.ps[:, 1, tt * 64:(tt + 1) * 64], small_t[:, tt * P:(tt + 1) * P], sq(m, "eye")[0:64, 0:64])
            last.then_inc(small_turned, 1)
            pe.wait_ge(small_out, 1)
            with pe.Fori(0, TRIPS) as i:
                for t in range(TILES):
                    j = (t // 2) % 2
                    if t % 2 == 0:
                        pe.wait_ge(low, i * CHUNKS + (t // 2 + 1))
                    pe.wait_ge(conv, i * TILES + (t + 1))
                    f = slice((t % 2) * P, (t % 2 + 1) * P)
                    products(pe, m.ps[:, t, :], [(wh[:, j, k, f], wl[:, j, k, f]) for k in range(KT)],
                             [(m.nh[:, k, :], m.nl[:, k, :]) for k in range(KT)]).then_inc(prod, 1)
            pe.wait_ge(dve_small, 1)
            pe.wait_ge(conv, N_CONV + 2)
            g = m.decay[:, :, 32:48]
            for n, mask in enumerate(("le", "ge", "gt", "lt")):
                last = pe.matmul(m.ps[:, 1, n * 64:(n + 1) * 64], sq(m, mask), g, start=True, stop=True)
            last.then_inc(gate_out, 1)

        @block.scalar
        def _(act):
            st = Steps(act, act_s)

            def split(c):
                act.wait_ge(w_in[c], 16)
                act.activation(wh[:, c, :, :], w[:, c, :, :], ACT.Copy).then_inc(high, 1)

            def first_weights():
                act.wait_ge(ws_in, 16)
                act.activation(wsh[:, :, :], ws[:, :, :], ACT.Copy).then_inc(small_high, 1)
                split(0)
                act.wait_ge(const_in, 48)

            norm.act(act, lambda tt: act.wait_ge(x_in[tt], 16), first_weights)
            split(1)
            act.wait_ge(small_prod, 1)
            act.activation(small_t[:, :], m.ps[0:64, 0, :], ACT.Copy).then_inc(small_staged, 1)
            act.wait_ge(small_turned, 1)
            act.activation(m.small[:, :, :], m.ps[:, 1, 0:TT * 64].rearrange("p (t n) -> p t n", n=64),
                           ACT.Copy).then_inc(small_out, 1)
            st.done(act.activation(tab[:, :], m.rowp[:, ROW_ALOG:ROW_ALOG + 48], ACT.Exp))
            act.wait_ge(dve_s, 3)
            st.done(act.activation(tmp[:, 2, :, :], tmp[:, 1, :, :], ACT.Exp))
            act.wait_ge(small_out, 1)
            st.done(act.activation(m.small[:, :, 48:64], m.small[:, :, 48:64], ACT.Sigmoid))

            def body(i, last):
                st.loop(0 if last else i, TILES)

                def silu(t):
                    hold(act, m, conv, i * TILES + (TILES + t + 1))
                    ct = m.ch[:, bass.ds(i * TILES + t, 1), :]
                    st.done(act.activation(ct, ct, ACT.Silu))

                for t in range(TILES):
                    hold(act, m, prod, i * TILES + (t + 1))
                    c = i * TILES + t
                    act.activation(m.ch[:, bass.ds(c, 1), :], m.ps[:, t:t + 1, :], ACT.Identity,
                                   bias=tap(c, 4), scale=tap(c, 2)).then_inc(taps0, 1)
                    if t % 2 == 1 and not (last and t >= TILES - 4):
                        j = (t // 2) % 2
                        act.wait_ge(w_in[j], i * 32 + (16 * ((t // 2 + 2) // 2) + 16))
                        act.activation(wh[:, j, :, :], w[:, j, :, :], ACT.Copy).then_inc(high, 1)
                    if t:
                        silu(t - 1)
                silu(TILES - 1)

            with act.Fori(0, TRIPS - 1) as i:
                body(i, False)
            st.end(TRIPS - 1)
            body(TRIPS - 1, True)
            act.wait_ge(gate_out, 1)
            act.activation(m.edk[:, :, :, :], m.ps[:, 1, 0:256].rearrange("p (a t n) -> p a t n", a=4, n=16),
                           ACT.Exp).then_inc(act_small, 1)

        @block.vector
        def _(dve):
            st = Steps(dve, dve_s)
            for tt in range(TT):
                dve.wait_ge(x_in[tt], 16)
            dve.wait_ge(const_in, 48)
            norm.dve(dve)
            dve.sem_inc(conv, TILES)
            bias = m.rowp[:, ROW_BIAS:ROW_BIAS + 48].unsqueeze(1).broadcast_to([P, TT, 48])
            z, nz, e, s, q = (tmp[:, n, :, :] for n in range(5))
            dve.wait_ge(small_out, 1)
            st.done(dve.tensor_tensor(z, m.small[:, :, 0:48], bias, ALU.add))
            st.done(dve.tensor_scalar(nz, z, -1.0, None, ALU.mult))
            st.done(dve.tensor_tensor(nz, nz, z, ALU.min))
            dve.wait_ge(act_s, 2)
            st.done(dve.tensor_scalar(nz, e, 2.0, None, ALU.add))
            st.done(dve.reciprocal(nz, nz))
            st.done(dve.tensor_tensor(s, e, nz, ALU.mult))
            st.done(dve.tensor_tensor(e, s, s, ALU.mult))
            co = log1p_coeffs()
            st.done(dve.tensor_scalar(q, e, co[-1], None, ALU.mult))
            for c in co[-2:0:-1]:
                st.done(dve.scalar_tensor_tensor(q, q, c, e, ALU.add, ALU.mult))
            st.done(dve.scalar_tensor_tensor(q, q, co[0], s, ALU.add, ALU.mult))
            st.done(dve.tensor_scalar(z, z, 0.0, None, ALU.max))
            st.done(dve.scalar_tensor_tensor(m.small[:, :, 0:48], q, 2.0, z, ALU.mult, ALU.add))
            st.done(dve.tensor_scalar(tab[:, :], tab[:, :], -1.0, None, ALU.mult))
            dve.tensor_tensor(m.decay[:, :, :], m.small[:, :, 0:48], tab[:, :].unsqueeze(1).broadcast_to([P, TT, 48]),
                              ALU.mult).then_inc(dve_small, 1)
            with dve.Fori(0, TRIPS) as i:
                st.loop(i, 2 * TILES)
                for t in range(TILES):
                    c = i * TILES + t
                    y = m.ch[:, bass.ds(c, 1), :].rearrange("p a (s l) -> p (a s) l", l=L)
                    x = m.ps[:, t, :].rearrange("p (s l) -> p s l", l=L)
                    dve.wait_ge(taps0, i * TILES + (t + 1))
                    for n, (k, lo, hi) in enumerate(((0, 2, 0), (1, 1, 0), (3, 0, 1))):
                        yy = y[:, :, lo:L - hi]
                        xx = x[:, :, 0:L - lo] if lo else x[:, :, hi:L]
                        op = dve.scalar_tensor_tensor(yy, xx, tap(c, k), yy, ALU.mult, ALU.add)
                        if n < 2:
                            st.done(op)
                        else:
                            op.then_inc(conv, 1)
            st.end(TRIPS)
            dve.wait_ge(act_small, 1)
            st.done(dve.tensor_scalar(m.ned[:, :, :, :], m.edk[:, 0:2, :, :], -1.0, None, ALU.mult))


CH_X, CH_B, CH_C, CH_Q, CH_K, CH_V = 0, 8, 12, 16, 24, 32


def turn_stage(nc, m):
    m.vt = m.ch[:, CH_X:CH_X + 8, :].rearrange("p (t a) n -> p t (a n)", t=TT)
    m.kt = m.ch[:, CH_V:CH_V + 8, :].rearrange("p (t a) n -> p t (a n)", t=TT)
    NQK = CH_V - CH_Q
    SLOTS = 4
    work = m.region(AT_WORK, AT_END - 4.25)
    s2 = work.take("squares_of", [P, SLOTS, T])
    norms = work.take("norms_of", [NQK, T])
    strip = work.take("column_strip", [P, 2 * NQK - 1])
    rows = work.take("row_selectors", [NQK, NQK, P])
    squared, summed, rooted, inverted, spread = (m.sem(x) for x in ("qk_squared", "qk_summed", "qk_rooted", "qk_inverted", "qk_spread"))
    scaled, turned, copied_a, copied_v = (m.sem(x) for x in ("qk_scaled", "turned", "turned_copied_act", "turned_copied_dve"))
    made, zeroed = m.sem("selectors_made"), m.sem("strip_zeroed")
    order = [(CH_X, m.xt), (CH_V, m.vt), (CH_K, m.kt)]
    HALF = 2
    with nc.Block() as block:

        @block.gpsimd
        def _(pool):
            pool.memset(strip[:, :], 0.0).then_inc(zeroed, 1)
            pool.wait_ge(zeroed, 1)
            pool.memset(strip[:, NQK - 1:NQK], 1.0).then_inc(made, 1)
            pool.tensor_copy(rows[:, :, :], sq(m, "eye")[0:NQK, 0:NQK].unsqueeze(2).broadcast_to([NQK, NQK, P])).then_inc(made, 1)

        @block.scalar
        def _(act):
            for k in range(NQK):
                if k >= SLOTS:
                    act.wait_ge(summed, k - SLOTS + 1)
                act.activation(s2[:, k % SLOTS, :], m.ch[:, CH_Q + k, :], ACT.Square).then_inc(squared, 1)
            act.wait_ge(summed, NQK)
            act.activation(norms[:, :], m.ps[0:NQK, 0, :], ACT.Sqrt, bias=m.eps[0:NQK, 0:1]).then_inc(rooted, 1)
            for n, (base, out) in enumerate(order):
                for tt in range(TT):
                    g = (n * TT + tt) * HALF
                    act.wait_ge(turned, g + 1)
                    act.activation(out[:, tt, 0:CW], m.ps[:, 4 + g % 4, :], ACT.Copy).then_inc(copied_a, 1)

        @block.tensor
        def _(pe):
            pe.wait_ge(made, 1)
            for k in range(NQK):
                pe.wait_ge(squared, k + 1)
                pe.matmul(m.ps[0:NQK, 0, :], strip[:, NQK - 1 - k:2 * NQK - 1 - k], s2[:, k % SLOTS, :], start=k == 0,
                          stop=k == NQK - 1).then_inc(summed, 1)

            def turn(n):
                base = order[n][0]
                for tt in range(TT):
                    for half in range(HALF):
                        g = (n * TT + tt) * HALF + half
                        if g >= 4:
                            pe.wait_ge(copied_v if half else copied_a, g // 2 - 1)
                        for a in range(4):
                            last = pe.transpose(m.ps[:, 4 + g % 4, a * P:(a + 1) * P],
                                                m.ch[:, base + half * 4 + a, tt * P:(tt + 1) * P], sq(m, "eye"))
                        last.then_inc(turned, 1)

            turn(0)
            turn(1)
            pe.wait_ge(made, 2)
            pe.wait_ge(inverted, 1)
            for k in range(NQK):
                if k >= SLOTS:
                    pe.wait_ge(scaled, k - SLOTS + 1)
                pe.matmul(m.ps[:, k % SLOTS, :], rows[:, k, :], norms[:, :], start=True, stop=True).then_inc(spread, 1)
            pe.wait_ge(scaled, NQK)
            turn(2)

        @block.vector
        def _(dve):
            def copies(n):
                out = order[n][1]
                for tt in range(TT):
                    g = (n * TT + tt) * HALF + 1
                    dve.wait_ge(turned, g + 1)
                    dve.tensor_copy(out[:, tt, CW:2 * CW], m.ps[:, 4 + g % 4, :]).then_inc(copied_v, 1)

            dve.wait_ge(rooted, 1)
            dve.reciprocal(norms[:, :], norms[:, :]).then_inc(inverted, 1)
            copies(0)
            copies(1)
            for k in range(NQK):
                dve.wait_ge(spread, k + 1)
                c = m.ch[:, CH_Q + k, :]
                scale = GDN_D ** -0.5 if k < NQK // 2 else 1.0
                dve.scalar_tensor_tensor(c, c, scale, m.ps[:, k % SLOTS, :], ALU.mult, ALU.mult).then_inc(scaled, 1)
            copies(2)


def ssd_stage(nc, m):
    regions = [m.region(AT_OG, AT_CH), m.region(AT_WORK, AT_END - 4.25)]
    e = [regions[1].take(f"mix{s}", [P, 2, 3, SSD_R, P]) for s in range(SEQS)]
    per = lambda name, shape: [regions[s].take(f"{name}{s}", shape) for s in range(SEQS)]
    sems = lambda name: [m.sem(f"ssd_{name}{s}") for s in range(SEQS)]
    bst = per("b_stage", [P, L])
    steps_h, steps_l = ([regions[s].take(f"decay_steps_{x}{s}", [P, TS, SSD_R, P], F32R) for s in range(SEQS)] for x in ("high", "low"))
    dec_h, dec_l = (regions[1].take(f"decay_{x}", [P, TT, 2 * SSD_H], F32R) for x in ("high", "low"))
    masks = regions[1].take("ssd_masks", [P, 3, P], F32R)
    mask_of = {name: masks[:, n, :] for n, name in enumerate(("gt", "lt", "ones"))}
    split_high, split_low = m.sem("decay_high"), m.sem("decay_low")
    sc, xd = per("masked_scores", [P, 2, 3, P]), per("x_dt", [P, 2, TS, SSD_R, SSD_P])
    staged, scored, stepped, summed, decayed = (sems(x) for x in ("staged", "scored", "steps_made", "summed", "decayed"))
    mixed, x_done, y_done, out_done = (sems(x) for x in ("mixed", "x_dt_done", "y_done", "out_done"))
    dve_s = m.sem("ssd_dve_steps")
    bank = lambda s, n: m.ps[:, 4 * s + n, :]
    with nc.Block() as block:

        @block.scalar
        def _(act):
            act.activation(dec_h[:, :, :], m.decay[:, :, 0:2 * SSD_H], ACT.Copy).then_inc(split_high, 1)
            for name, mask in mask_of.items():
                last = act.activation(mask, sq(m, name), ACT.Copy)
            last.then_inc(split_high, 1)
            with act.Fori(0, SSD_G) as g:
                for s in range(SEQS):
                    hold(act, m, y_done[s], g + 1)
                    act.activation(bst[s][:, :], m.ch[:, bass.ds(g + CH_B, 1), s * L:(s + 1) * L], ACT.Copy).then_inc(staged[s], 1)
                for d in range(2):
                    for s in range(SEQS):
                        act.wait_ge(summed[s], g * 2 + (d + 2))
                        for b in range(3):
                            last = act.activation(e[s][:, d, b, :, :].rearrange("p h c -> p (h c)"), bank(s, 1 + b), ACT.Exp)
                        last.then_inc(decayed[s], 1)

        @block.gpsimd
        def _(pool):
            pool.wait_ge(split_high, 1)
            pool.wait_ge(split_low, 1)
            with pool.Fori(0, SSD_G) as g:
                for d in range(2):
                    mask = sq(m, "ge" if d else "le").unsqueeze(1).broadcast_to([P, SSD_R, P])
                    for s in range(SEQS):
                        hold(pool, m, summed[s], g * 2 + (d + 1))
                        for t in range(TS):
                            for dec, steps in ((dec_h, steps_h), (dec_l, steps_l)):
                                col = bits32(dec[:, TS * s + t, bass.ds(g * SSD_R + d * SSD_H, SSD_R)]).unsqueeze(2)
                                last = pool.tensor_tensor(steps[s][:, t, :, :], col.broadcast_to([P, SSD_R, P]), mask, ALU.mult)
                        last.then_inc(stepped[s], 1)

        @block.tensor
        def _(pe):
            for s in range(SEQS):
                pe.sem_inc(summed[s], 1)
                pe.sem_inc(y_done[s], 1)
            pe.wait_ge(split_high, 2)
            with pe.Fori(0, SSD_G) as g:
                for s in range(SEQS):
                    pe.wait_ge(staged[s], g + 1)
                    pe.wait_ge(out_done[s], g + 1)
                    for t in range(TS):
                        last = pe.matmul(bank(s, 0)[:, t * L:(t + 1) * L], bst[s][:, t * P:(t + 1) * P],
                                         m.ch[:, bass.ds(g + CH_C, 1), s * L:(s + 1) * L], start=True, stop=True)
                    last.then_inc(scored[s], 1)
                for d in range(2):
                    before = "lt" if d else "gt"
                    for s in range(SEQS):
                        pe.wait_ge(stepped[s], g * 2 + (d + 1))
                        pe.wait_ge(decayed[s], g * 2 + (d + 1))
                        near = [[x[s][:, n, :, :].rearrange("p h c -> p (h c)") for x in (steps_h, steps_l)] for n in range(TS)]
                        far = [x[:, TS * s + d, bass.ds(g * SSD_R + d * SSD_H, SSD_R)].unsqueeze(2).broadcast_to([P, SSD_R, P])
                               for x in (dec_h, dec_l)]
                        for n, terms in ((1, [(before, near[0])]), (3, [(before, near[1])]), (2, [(before, far), ("ones", near[1 - d])])):
                            for k, (mask, parts) in enumerate(terms):
                                for p in range(2):
                                    last = pe.matmul(bank(s, n), mask_of[mask], parts[p], start=k + p == 0, stop=k + p == len(terms))
                        last.then_inc(summed[s], 1)
                for s in range(SEQS):
                    pe.wait_ge(mixed[s], g * 2 + 2)
                    pe.wait_ge(x_done[s], g + 1)
                    for t in range(TS):
                        terms = [(0, 2 * t, t), (1, 2 * t, t), ((0, 1, 0) if t else (1, 1, 1))]
                        for h in range(SSD_R):
                            o = bank(s, 0)[:, (t * SSD_R + h) * SSD_P:(t * SSD_R + h + 1) * SSD_P]
                            for n, (d, b, src) in enumerate(terms):
                                last = pe.matmul(o, e[s][:, d, b, h, :], xd[s][:, d, src, h, :], start=n == 0, stop=n == 2)
                    last.then_inc(y_done[s], 1)

        @block.vector
        def _(dve):
            st = Steps(dve, dve_s)
            dve.wait_ge(split_high, 1)
            dve.tensor_tensor(dec_l[:, :, :], m.decay[:, :, 0:2 * SSD_H], bits32(dec_h[:, :, :]), ALU.subtract).then_inc(split_low, 1)
            for s in range(SEQS):
                dve.sem_inc(out_done[s], 1)
                dve.sem_inc(decayed[s], 1)
            with dve.Fori(0, SSD_G) as g:
                st.loop(g, 2 * SEQS)
                xs = [m.xt[:, TS * s:TS * s + TS, bass.ds(g * (SSD_R * SSD_P), SSD_R * SSD_P)]
                      .rearrange("p t (h c) -> p t h c", c=SSD_P) for s in range(SEQS)]
                for s in range(SEQS):
                    dve.wait_ge(scored[s], g + 1)
                    le, ge = sq(m, "le"), sq(m, "ge")
                    blk = lambda src, dst: bank(s, 0)[:, src * L + dst * P:src * L + dst * P + P]
                    for t in range(TS):
                        dve.tensor_tensor(sc[s][:, 0, 2 * t, :], blk(t, t), le, ALU.mult)
                        dve.tensor_tensor(sc[s][:, 1, 2 * t, :], blk(t, t), ge, ALU.mult)
                    dve.tensor_copy(sc[s][:, 0, 1, :], blk(0, 1))
                    st.done(dve.tensor_copy(sc[s][:, 1, 1, :], blk(1, 0)))
                    dve.wait_ge(y_done[s], g + 1)
                    for d in range(2):
                        dt = m.small[:, TS * s:TS * s + TS, bass.ds(g * SSD_R + d * SSD_H, SSD_R)].unsqueeze(3)
                        last = dve.tensor_tensor(xd[s][:, d, :, :, :], xs[s], dt.broadcast_to([P, TS, SSD_R, SSD_P]), ALU.mult)
                    last.then_inc(x_done[s], 1)
                for d in range(2):
                    for s in range(SEQS):
                        dve.wait_ge(decayed[s], g * 2 + (d + 2))
                        for b in range(3):
                            last = dve.tensor_tensor(e[s][:, d, b, :, :], e[s][:, d, b, :, :],
                                                     sc[s][:, d, b, :].unsqueeze(1).broadcast_to([P, SSD_R, P]), ALU.mult)
                        last.then_inc(mixed[s], 1)
                for s in range(SEQS):
                    skip = m.rowp[:, bass.ds(g * SSD_R + ROW_D, SSD_R)].unsqueeze(1).unsqueeze(3)
                    st.done(dve.tensor_tensor(xs[s], xs[s], skip.broadcast_to([P, TS, SSD_R, SSD_P]), ALU.mult))
                    dve.wait_ge(y_done[s], g + 2)
                    y = bank(s, 0).rearrange("p (t h c) -> p t h c", t=TS, h=SSD_R)
                    dve.tensor_tensor(xs[s], y, xs[s], ALU.add).then_inc(out_done[s], 1)
            st.end(SSD_G)


def gdn_stage(nc, m):
    NL = len(LEVELS)
    HEADS = 2
    TRIPS = GDN_H // HEADS
    lanes = [(hh, s) for hh in range(HEADS) for s in range(SEQS)]
    U = range(len(lanes))
    DVE_LANES = (0, 1)
    spare = m.region(AT_CH + 2 * CH_B, AT_CH + 2 * CH_Q)
    work = m.region(AT_WORK, AT_END - 4.25)

    def per(name, shape):
        size = 4 * int(np.prod(shape[1:]))
        return [(spare if spare.at + size <= spare.end else work).take(f"gdn_{name}{u}", shape) for u in U]

    halves = work.take("gdn_halves", [P, NL, P])
    sems = lambda name: [m.sem(f"gdn_{name}{u}") for u in U]
    kq = per("kq", [P, 2, L])
    steps, e, at, qk = (per(x, [P, 4, P]) for x in ("steps", "decay", "a_t", "qk"))
    vn, kd, first_part, invs = per("v_new", [P, 4, P]), per("k_dec", [P, 2, P]), per("first_part", [P, 2, P]), per("inverse_t", [P, 2, P])
    items = lambda x: x[:, :, :].rearrange("p (d c) n -> p d c n", d=2)
    both = lambda x: x[:, 0:2, :]
    am, y, invt = [x[:, 0:2, :] for x in e], [x[:, 2:4, :] for x in e], e
    second_part, st8 = [x[:, 2:4, :] for x in at], [x[:, 2:4, :] for x in at]
    z, oq = first_part, invs
    (staged, kq_done, stepped, summed, decayed, weighed, a_made, levelled, inv_done, turned, first_done, second_done, y_done, y_copied,
     masked, qk_copied, p_done, split_done, u_done, vn_done, kd_done, s_done, s_copied, ks_done, z_done, w_done, o_done, out_done) = (
        sems(x) for x in ("staged", "kq", "steps_made", "summed", "decayed", "weighed", "a_made", "levelled",
                          "inv_t_done", "inv_turned", "first_part", "second_part", "y_done", "y_copied", "masked", "qk_copied", "p_done", "inv_split",
                          "tv_done", "v_new_done", "k_dec_done", "state_done", "state_copied", "ks_done", "z_done", "tz_done",
                          "o_done", "out_done"))
    dve_s, halves_in = m.sem("gdn_dve_steps"), m.sem("gdn_halves_loaded")
    bank = lambda u, n: m.ps[:, 2 * u + n, :]
    bank4 = lambda u, n: m.ps[:, 2 * u + n, :].rearrange("p (i c) -> p i c", c=P)
    first = (0, 3)
    second = (1, 2)
    pair = lambda x: x.unsqueeze(1).broadcast_to([P, TS, P])
    with nc.Block() as block:

        @block.sync
        def _(sp):
            sp.dma_start(halves[:, :, :], m.ins["halves"].rearrange("p (n c) -> p n c", c=P)).then_inc(halves_in, 16)

        @block.scalar
        def _(act):
            with act.Fori(0, TRIPS) as i:
                for u in U:
                    hh, s = lanes[u]
                    hold(act, m, ks_done[u], i + 1)
                    for n, base in enumerate((CH_K, CH_Q)):
                        last = act.activation(kq[u][:, n:n + 1, :], m.ch[:, bass.ds(i * HEADS + (hh + base), 1), s * L:(s + 1) * L],
                                              ACT.Copy)
                    last.then_inc(staged[u], 1)
                for u in U:
                    act.wait_ge(summed[u], i + 2)
                    act.activation(e[u][:, :, :], bank4(u, 1), ACT.Exp).then_inc(decayed[u], 1)
                    act.wait_ge(kq_done[u], i + 1)
                    kk = bank(u, 0).rearrange("p (c a n) -> p c a n", c=2, a=2)
                    act.activation(both(vn[u]), kk[:, :, 1, :], ACT.Copy).then_inc(qk_copied[u], 1)
                for u in U:
                    hh, s = lanes[u]
                    for n, it in enumerate(first):
                        t = TS * s + it % 2
                        scale = m.edk[:, 2 + n, t, bass.ds(i * HEADS + (hh + n * GDN_H), 1)]
                        last = act.activation(kd[u][:, n, :], m.kt[:, t, bass.ds(i * (HEADS * P) + hh * P, P)], ACT.Copy, scale=scale)
                    last.then_inc(kd_done[u], 1)
                for lv in range(NL):
                    for u in U:
                        act.wait_ge(y_done[u], i * NL + (lv + 1))
                        act.activation(y[u], bank4(u, 0)[:, 2:4, :], ACT.Copy).then_inc(y_copied[u], 1)
                def new_values(u, n, it):
                    beta = m.small[:, TS * lanes[u][1] + it % 2, bass.ds(i * HEADS + (48 + lanes[u][0] + it // 2 * GDN_H), 1)]
                    return act.activation(vn[u][:, it, :], bank4(u, 1)[:, n, :], ACT.Copy, scale=beta)

                for u in U:
                    hold(act, m, weighed[u], i + 1)
                    hold(act, m, u_done[u], i + 1)
                    for n, it in enumerate(first):
                        last = new_values(u, n, it)
                    last.then_inc(vn_done[u], 1)
                for u in U:
                    act.wait_ge(s_done[u], i + 1)
                    act.activation(st8[u], both(bank4(u, 0)), ACT.Copy).then_inc(s_copied[u], 1)
                for u in U:
                    hold(act, m, w_done[u], i + 1)
                    for n, it in enumerate(second):
                        last = new_values(u, 2 + n, it)
                    last.then_inc(vn_done[u], 1)

        @block.gpsimd
        def _(pool):
            pool.wait_ge(halves_in, 16)
            with pool.Fori(0, TRIPS) as i:
                for u in U:
                    hh, s = lanes[u]
                    hold(pool, m, summed[u], i + 1)
                    for d in range(2):
                        g = m.decay[:, TS * s:TS * s + TS, bass.ds(i * HEADS + (32 + hh + d * GDN_H), 1)].broadcast_to([P, TS, P])
                        last = pool.tensor_tensor(steps[u][:, 2 * d:2 * d + 2, :], g, pair(sq(m, "ge" if d else "le")), ALU.mult)
                    last.then_inc(stepped[u], 1)

                def level(u, b):
                    pool.tensor_tensor(am[u], both(at[u]), pair(sq(m, f"lvl{b}")), ALU.mult).then_inc(levelled[u], 1)

                for u in U:
                    pool.wait_ge(decayed[u], i + 1)
                    pool.tensor_tensor(items(qk[u]), items(e[u]), sq_pair(m, "le", 2), ALU.mult).then_inc(masked[u], 1)
                for u in U:
                    pool.wait_ge(a_made[u], i + 1)
                    level(u, 1)
                for u in U:
                    pool.wait_ge(inv_done[u], i * (NL + 1) + 1)
                    level(u, LEVELS[0])
                for lv in range(NL):
                    for u in U:
                        pool.wait_ge(inv_done[u], i * (NL + 1) + (lv + 1))
                        pool.tensor_tensor(second_part[u], invs[u][:, :, :], pair(halves[:, lv, :]), ALU.mult).then_inc(second_done[u], 1)
                    if lv < NL - 1:
                        for u in U:
                            if u not in DVE_LANES:
                                pool.wait_ge(y_done[u], i * NL + (lv + 1))
                                level(u, LEVELS[lv + 1])

        @block.vector
        def _(dve):
            st = Steps(dve, dve_s)
            for u in U:
                dve.sem_inc(out_done[u], 1)
            dve.wait_ge(halves_in, 16)
            with dve.Fori(0, TRIPS) as i:
                st.loop(i, len(lanes))
                beta = lambda u, it: m.small[:, TS * lanes[u][1] + it % 2, bass.ds(i * HEADS + (48 + lanes[u][0] + it // 2 * GDN_H), 1)]
                for u in U:
                    dve.wait_ge(masked[u], i + 1)
                    dve.wait_ge(qk_copied[u], i + 1)
                    kk = bank(u, 0).rearrange("p (c a n) -> p c a n", c=2, a=2)
                    for it in range(4):
                        last = dve.scalar_tensor_tensor(at[u][:, it, :], qk[u][:, it, :], beta(u, it), kk[:, it % 2, 0, :],
                                                        ALU.mult, ALU.mult)
                    st.done(last)
                    dve.tensor_tensor(both(at[u]), both(at[u]), at[u][:, 2:4, :], ALU.add).then_inc(a_made[u], 1)
                for u in U:
                    dve.wait_ge(levelled[u], i * (NL + 1) + 1)
                    dve.tensor_tensor(invs[u][:, :, :], pair(sq(m, "eye")), am[u], ALU.subtract).then_inc(inv_done[u], 1)
                for lv in range(NL):
                    for u in U:
                        dve.wait_ge(turned[u], i * NL + (lv + 1))
                        dve.tensor_tensor(first_part[u][:, :, :], both(bank4(u, 0)), pair(halves[:, lv, :]), ALU.mult).then_inc(first_done[u], 1)
                    for u in U:
                        if u in DVE_LANES and lv < NL - 1:
                            dve.wait_ge(y_done[u], i * NL + (lv + 1))
                            dve.tensor_tensor(am[u], both(at[u]), pair(sq(m, f"lvl{LEVELS[lv + 1]}")), ALU.mult).then_inc(levelled[u], 1)
                        if u == lv - 1:
                            for d in range(2):
                                q = qk[u][:, 2 * d:2 * d + 2, :]
                                last = dve.tensor_tensor(q, q, both(vn[u]), ALU.mult)
                            last.then_inc(weighed[u], 1)
                    for u in U:
                        dve.wait_ge(p_done[u], i * NL + (lv + 1))
                        dve.tensor_tensor(invs[u][:, :, :], invs[u][:, :, :], both(bank4(u, 1)), ALU.subtract).then_inc(inv_done[u], 1)
                for u in U:
                    dve.wait_ge(inv_done[u], (i + 1) * (NL + 1))
                    dve.tensor_tensor(invt[u][:, 0:2, :], invs[u][:, :, :], pair(sq(m, "le")), ALU.mult)
                    dve.tensor_tensor(invt[u][:, 2:4, :], invs[u][:, :, :], pair(sq(m, "ge")), ALU.mult).then_inc(split_done[u], 1)
                for u in U:
                    hh, s = lanes[u]
                    if u == 0:
                        for w in U:
                            dve.wait_ge(split_done[w], i + 1)
                    dve.wait_ge(ks_done[u], i + 2)
                    for n, it in enumerate(second):
                        t, c = TS * s + it % 2, bass.ds(i * HEADS + (hh + n * GDN_H), 1)
                        ks = bank4(u, 0)
                        dve.scalar_tensor_tensor(z[u][:, n, :], ks[:, 2 * n, :], m.ned[:, n, t, c],
                                                 m.vt[:, t, bass.ds(i * (HEADS * P) + hh * P, P)], ALU.mult, ALU.add)
                        last = dve.tensor_scalar(oq[u][:, it % 2, :], ks[:, 2 * n + 1, :], m.edk[:, n, t, c], None, ALU.mult)
                    last.then_inc(z_done[u], 1)
                for u in U:
                    hh, s = lanes[u]
                    dve.wait_ge(o_done[u], i + 1)
                    dve.tensor_tensor(m.og[:, TS * s:TS * s + TS, bass.ds(i * (HEADS * P) + hh * P, P)], both(bank4(u, 0)),
                                      oq[u][:, :, :], ALU.add).then_inc(out_done[u], 1)
            st.end(TRIPS)

        @block.tensor
        def _(pe):
            for u in U:
                pe.sem_inc(summed[u], 1)
                pe.sem_inc(ks_done[u], 1)
            with pe.Fori(0, TRIPS) as i:
                for u in U:
                    pe.wait_ge(staged[u], i + 1)
                    pe.wait_ge(out_done[u], i + 1)
                    for c in range(TS):
                        last = pe.matmul(bank(u, 0)[:, c * L:(c + 1) * L].rearrange("p (a n) -> p a n", a=2),
                                         kq[u][:, 0, c * P:(c + 1) * P], kq[u][:, :, c * P:(c + 1) * P], start=True, stop=True)
                    last.then_inc(kq_done[u], 1)
                    pe.wait_ge(stepped[u], i + 1)
                    for d in range(2):
                        last = pe.matmul(bank(u, 1)[:, d * L:(d + 1) * L], sq(m, "lt" if d else "gt"),
                                         steps[u][:, 2 * d:2 * d + 2, :].rearrange("p c n -> p (c n)"), start=True, stop=True)
                    last.then_inc(summed[u], 1)
                for u in U:
                    pe.wait_ge(qk_copied[u], i + 1)
                for lv in range(NL):
                    for u in U:
                        pe.wait_ge(inv_done[u], i * (NL + 1) + (lv + 1))
                        for c in range(TS):
                            last = pe.transpose(bank4(u, 0)[:, c, :], invs[u][:, c, :], sq(m, "eye"))
                        last.then_inc(turned[u], 1)
                    for u in U:
                        pe.wait_ge(first_done[u], i * NL + (lv + 1))
                        pe.wait_ge(levelled[u], i * (NL + 1) + (lv + 2))
                        for c in range(TS):
                            last = pe.matmul(bank4(u, 0)[:, 2 + c, :], am[u][:, c, :], first_part[u][:, c, :], start=True, stop=True)
                        last.then_inc(y_done[u], 1)
                    for u in U:
                        pe.wait_ge(y_copied[u], i * NL + (lv + 1))
                        pe.wait_ge(second_done[u], i * NL + (lv + 1))
                        for c in range(TS):
                            last = pe.matmul(bank4(u, 1)[:, c, :], y[u][:, c, :], second_part[u][:, c, :], start=True, stop=True)
                        last.then_inc(p_done[u], 1)
                for u in U:
                    hh, s = lanes[u]
                    pe.wait_ge(split_done[u], i + 1)
                    for n, it in enumerate(first):
                        last = pe.matmul(bank4(u, 1)[:, n, :], invt[u][:, it, :], m.vt[:, TS * s + it % 2, bass.ds(i * (HEADS * P) + hh * P, P)],
                                         start=True, stop=True)
                    last.then_inc(u_done[u], 1)
                for u in U:
                    pe.wait_ge(vn_done[u], i * 2 + 1)
                    pe.wait_ge(kd_done[u], i + 1)
                    for n, it in enumerate(first):
                        last = pe.matmul(bank4(u, 0)[:, n, :], kd[u][:, n, :], vn[u][:, it, :], start=True, stop=True)
                    last.then_inc(s_done[u], 1)
                for u in U:
                    pe.wait_ge(s_copied[u], i + 1)
                    for n, it in enumerate(second):
                        c = it % 2
                        for a in range(2):
                            last = pe.matmul(bank4(u, 0)[:, 2 * n + a, :], kq[u][:, a, c * P:(c + 1) * P], st8[u][:, n, :],
                                             start=True, stop=True)
                    last.then_inc(ks_done[u], 1)
                for u in U:
                    pe.wait_ge(z_done[u], i + 1)
                    for n, it in enumerate(second):
                        last = pe.matmul(bank4(u, 1)[:, 2 + n, :], invt[u][:, it, :], z[u][:, n, :], start=True, stop=True)
                    last.then_inc(w_done[u], 1)
                for u in U:
                    pe.wait_ge(vn_done[u], i * 2 + 2)
                    pe.wait_ge(weighed[u], i + 1)
                    for c in range(TS):
                        for d in range(2):
                            last = pe.matmul(bank4(u, 0)[:, c, :], qk[u][:, 2 * d + c, :], vn[u][:, 2 * d + c, :], start=d == 0, stop=d == 1)
                    last.then_inc(o_done[u], 1)


class Stream:

    def __init__(self, m, raw, split, tag, chunks):
        self.m, self.chunks = m, chunks
        self.w = raw.take(f"{tag}_slots", [P, 2, KT // 2, CW])
        self.wh = split.take(f"{tag}_high", [P, 2, KT // 2, CW], F32R)
        self.wl = split.take(f"{tag}_low", [P, 2, KT // 2, CW], F32R)
        self.loaded = [m.sem(f"{tag}_slot{j}_loaded") for j in range(2)]
        self.high_done, self.low_done, self.used, self.prod = (m.sem(f"{tag}_{x}") for x in ("high", "low", "first_half_used", "products"))

    def sp(self, sp):
        for n in range(2 * len(self.chunks)):
            j, half = n % 2, KT // 2 * CW
            if n >= 2:
                sp.wait_ge(self.low_done, n - 1)
            src = self.chunks[n // 2][:, j * half:(j + 1) * half]
            sp.dma_start(self.w[:, j, :, :], src.rearrange("p (k n) -> p k n", n=CW)).then_inc(self.loaded[j], 16)

    def high(self, act, n):
        if n >= 2 * len(self.chunks):
            return
        j, pair = n % 2, n // 2
        act.wait_ge(self.loaded[j], 16 * (pair + 1))
        if pair:
            act.wait_ge(self.prod if j else self.used, 4 * pair if j else pair)
        act.activation(self.wh[:, j, :, :], self.w[:, j, :, :], ACT.Copy).then_inc(self.high_done, 1)

    def pool(self, pool):
        for n in range(2 * len(self.chunks)):
            j = n % 2
            pool.wait_ge(self.high_done, n + 1)
            pool.tensor_tensor(self.wl[:, j, :, :], self.w[:, j, :, :], bits32(self.wh[:, j, :, :]),
                               ALU.subtract).then_inc(self.low_done, 1)

    def act(self, act, pair, consume):
        self.high(act, 2 * pair + 2)
        consume()
        self.high(act, 2 * pair + 3)

    def pe(self, pe, pair, banks, free, x, token_major, ready=lambda kt: None):
        m = self.m
        for j in range(2):
            pe.wait_ge(self.low_done, 2 * pair + j + 1)
            for f in range(4):
                if j == 0:
                    free(f)
                c = slice(f * P, (f + 1) * P)
                for k in range(KT // 2):
                    kt = j * (KT // 2) + k
                    if f == 0:
                        ready(kt)
                    if token_major:
                        a, b = [y[:, kt, c] for y in x], [w[:, j, k, :] for w in (self.wh, self.wl)]
                    else:
                        a, b = [w[:, j, k, c] for w in (self.wh, self.wl)], [y[:, kt, :] for y in x]
                    for n, (u, v) in enumerate(((0, 0), (0, 1), (1, 0))):
                        last = pe.matmul(m.ps[:, banks + f, :], a[u], b[v], start=kt == 0 and n == 0,
                                         stop=kt == KT - 1 and n == 2)
                if j:
                    last.then_inc(self.prod, 1)
            if j == 0:
                last.then_inc(self.used, 1)


def merge_stage(nc, m):
    G = (SSD_G, GDN_H)
    chunks = [m.ins["w_gates"][n] for n in (0, 1, 4, 5)]
    for a, name in enumerate(("w_ssd_out", "w_gdn_out")):
        for n in range(2):
            chunks += [m.ins[name][n], m.ins["w_gates"][4 * a + 2 + n]]
    chunks += [m.ins["w_out"][n] for n in range(2)]
    y = (m.xt, m.og)
    over = m.region(AT_XT, AT_CH)
    mh, ml = over.take("merged_high", [P, KT, T], F32R), over.take("merged_low", [P, KT, T], F32R)
    r = m.region(AT_CH, AT_END)
    yh, yl = r.take("mixer_high", [P, KT, T], F32R), r.take("mixer_low", [P, KT, T], F32R)
    mT = r.take("merged", [P, KT, T])
    zt = r.take("silu_z", [P, 4, CW])
    sqs = r.take("mixer_squares", [P, 2, D])
    sg = r.take("sig_gate", [P, 4, CW])
    ss = r.take("mixer_stat", [P, 2, TT, 8])
    stream = Stream(m, r, r, "merge", chunks)
    prod = stream.prod
    (silu, gated, squared, reduced, meaned, rooted, dve_s, scaled, turned, t_high, t_out, sig, mixed, m_high, m_low, added) = (
        m.sem(f"merge_{x}") for x in ("silu", "z_multiplied", "squared", "reduced", "meaned", "rooted", "dve_steps", "scaled",
                                      "turned", "turned_high", "turned_low", "gate_sigmoid", "mixed", "merged_high",
                                      "merged_low", "added"))
    n_x = (m.nh, m.nl)
    FIRST = (4, 8)
    with nc.Block() as block:

        @block.sync
        def _(sp):
            stream.sp(sp)

        @block.gpsimd
        def _(pool):
            stream.pool(pool)

        @block.tensor
        def _(pe):
            for p in range(4):
                stream.pe(pe, p, 4 * (p % 2), lambda tt: p < 2 or pe.wait_ge(silu, 4 * (p - 2) + tt + 1), n_x, True)
            for a in range(2):
                for kt in range(KT):
                    if a == 0:
                        pe.wait_ge(silu, 9 + kt)
                    elif kt == 0:
                        pe.wait_ge(mixed, 8)
                    if kt == 0:
                        pe.wait_ge(scaled, TT * (a + 1))
                    for tt in range(TT):
                        last = pe.transpose(m.ps[:, kt, tt * P:(tt + 1) * P], y[a][:, tt, kt * P:(kt + 1) * P], sq(m, "eye"))
                    last.then_inc(turned, 1)
                for n in range(2):
                    for gate in range(2):
                        p = FIRST[a] + 2 * n + gate

                        def free(f):
                            if n == 0:
                                pe.wait_ge(t_out, KT * a + 4 * gate + f + 1)
                            else:
                                pe.wait_ge(sig if gate else mixed, 4 * (2 * a) + f + 1)
                        turned_in = lambda kt: n or gate or pe.wait_ge(t_out, KT * a + kt + 1)
                        stream.pe(pe, p, 4 * gate, free, n_x if gate else (yh, yl), False, turned_in)

            def free_out(tt, p):
                if tt == 0:
                    pe.wait_ge(m_low, KT)
                if p == 13:
                    pe.wait_ge(sig, 16)
            for p in (12, 13):
                stream.pe(pe, p, 4 * (p - 12), lambda tt: free_out(tt, p), (mh, ml), True)

        @block.scalar
        def _(act):
            def squares(a, first):
                for tt in range(TT):
                    n = first + tt
                    if n >= 2:
                        act.wait_ge(reduced, n - 1)
                    act.activation(sqs[:, tt % 2, :], y[a][:, tt, :], ACT.Square).then_inc(squared, 1)

            def z(p):
                for tt in range(TT):
                    g = 4 * p + tt
                    act.wait_ge(prod, g + 1)
                    if g >= 4:
                        act.wait_ge(gated, g - 3)
                    act.activation(zt[:, tt, :], m.ps[:, 4 * (p % 2) + tt, :], ACT.Silu).then_inc(silu, 1)

            def sigmoids(p, k):
                for f in range(4):
                    act.wait_ge(prod, 4 * p + f + 1)
                    if k:
                        act.wait_ge(mixed, 4 * (k - 1) + f + 1)
                    act.activation(sg[:, f, :], m.ps[:, 4 + f, :], ACT.Sigmoid).then_inc(sig, 1)

            stream.high(act, 0)
            stream.high(act, 1)
            squares(1, 0)
            for p in range(2):
                stream.act(act, p, lambda: z(p))
            act.wait_ge(gated, 8)
            squares(0, TT)
            act.wait_ge(meaned, 1)
            act.activation(ss[:, :, :, :], ss[:, :, :, :], ACT.Sqrt).then_inc(rooted, 1)
            for p in range(2, 4):
                stream.act(act, p, lambda: z(p))
            for a in range(2):
                for kt in range(KT):
                    act.wait_ge(turned, KT * a + kt + 1)
                    col = COL_GDNN if a else COL_SSDN + kt
                    act.activation(yh[:, kt, :], m.ps[:, kt, :], ACT.Copy, scale=m.colp[:, col:col + 1]).then_inc(t_high, 1)
                for n in range(2):
                    p = FIRST[a] + 2 * n
                    stream.act(act, p, lambda: None)
                    stream.act(act, p + 1, lambda: sigmoids(p + 1, 2 * a + n))
                    if a:
                        for f in range(4):
                            act.wait_ge(mixed, 8 + 4 * n + f + 1)
                            act.activation(mh[:, 4 * n + f, :], mT[:, 4 * n + f, :], ACT.Copy).then_inc(m_high, 1)
            stream.act(act, 12, lambda: None)

        @block.vector
        def _(dve):
            st = Steps(dve, dve_s)

            def reduce(a, first):
                for tt in range(TT):
                    dve.wait_ge(squared, first + tt + 1)
                    dve.tensor_reduce(ss[:, a, tt, 0:G[a]], sqs[:, tt % 2, :].rearrange("p (g c) -> p g c", g=G[a]),
                                      AX.X, ALU.add).then_inc(reduced, 1)

            def times_z(a):
                for g in range(8 * a, 8 * a + 8):
                    dve.wait_ge(silu, g + 1)
                    n = (g // 4) % 2
                    v = y[a][:, g % 4, n * CW:(n + 1) * CW]
                    dve.tensor_tensor(v, v, zt[:, g % 4, :], ALU.mult).then_inc(gated, 1)

            def scale(a):
                dve.wait_ge(gated, 8 * (a + 1))
                for tt in range(TT):
                    v = y[a][:, tt, :].rearrange("p (g c) -> p g c", g=G[a])
                    dve.tensor_tensor(v, v, ss[:, a, tt, 0:G[a]].unsqueeze(2).broadcast_to([P, G[a], D // G[a]]),
                                      ALU.mult).then_inc(scaled, 1)

            st.done(dve.memset(ss[:, :, :, :], 1.0))
            reduce(1, 0)
            times_z(0)
            reduce(0, TT)
            dve.wait_ge(reduced, 2 * TT)
            for a in range(2):
                last = dve.tensor_scalar(ss[:, a, :, 0:G[a]], ss[:, a, :, 0:G[a]], G[a] / D, EPS, ALU.mult, ALU.add)
            last.then_inc(meaned, 1)
            dve.wait_ge(rooted, 1)
            st.done(dve.reciprocal(ss[:, :, :, :], ss[:, :, :, :]))
            scale(0)
            times_z(1)
            for a in range(2):
                for kt in range(KT):
                    dve.wait_ge(t_high, KT * a + kt + 1)
                    col = COL_GDNN if a else COL_SSDN + kt
                    dve.scalar_tensor_tensor(yl[:, kt, :], m.ps[:, kt, :], m.colp[:, col:col + 1], bits32(yh[:, kt, :]),
                                             ALU.mult, ALU.subtract).then_inc(t_out, 1)
                if a == 0:
                    scale(1)
                for n in range(2):
                    for f in range(4):
                        o = mT[:, 4 * n + f, :]
                        dve.wait_ge(sig, 4 * (2 * a + n) + f + 1)
                        if a == 0:
                            dve.tensor_tensor(o, m.ps[:, f, :], sg[:, f, :], ALU.mult).then_inc(mixed, 1)
                        else:
                            st.done(dve.tensor_tensor(sg[:, f, :], m.ps[:, f, :], sg[:, f, :], ALU.mult))
                            dve.tensor_tensor(o, o, sg[:, f, :], ALU.add).then_inc(mixed, 1)
                    if a:
                        for f in range(4):
                            dve.wait_ge(m_high, 4 * n + f + 1)
                            dve.tensor_tensor(ml[:, 4 * n + f, :], mT[:, 4 * n + f, :], bits32(mh[:, 4 * n + f, :]),
                                              ALU.subtract).then_inc(m_low, 1)
            for n in range(2):
                for tt in range(TT):
                    dve.wait_ge(prod, 4 * (12 + n) + tt + 1)
                    v = m.h[:, tt, n * CW:(n + 1) * CW]
                    dve.tensor_tensor(v, v, m.ps[:, 4 * n + tt, :], ALU.add).then_inc(added, 1)


def expert_stages(nc, m):
    g_dense = nc.dram_tensor("g_dense", (PEER_K, P, T), F32, kind="Internal").ap()
    a_dense = nc.dram_tensor("a_dense", (PEER_K, P, T), F32, kind="Internal").ap()
    m.scores = m.region(AT_SCORES, AT_SCORES + 32).take("key_scores", [P, TT, NHZ, PEER_K])
    down = DownLoads(nc, m, g_dense, a_dense)
    for stage, args in ((query_stage, ()), (up_stage, (g_dense, a_dense, down)), (down_stage, (down,))):
        stage(nc, m, *args)
        end_stage(nc, m)


def query_stage(nc, m):
    r = m.region(AT_SCORES + 32, AT_END)
    norm = NormT(nc, m, r, "ffn_norm", COL_FFN)
    qT = r.take("queries", [P, NHZ, T])
    keys = r.take("keys", [P, NHZ, PEER_K])
    q_out, scored, s_out, keys_in = (m.sem(f"query_{x}") for x in ("copied", "scored", "scores_out", "keys_in"))
    stream = Stream(m, r, r, "query", [m.ins["peer_query"][n] for n in range(4)])
    with nc.Block() as block:

        @block.sync
        def _(sp):
            sp.dma_start(keys[:, :, :], m.ins["peer_keys"].rearrange("p (a k) -> p a k", k=PEER_K)).then_inc(keys_in, 16)
            stream.sp(sp)

        @block.gpsimd
        def _(pool):
            stream.pool(pool)

        @block.tensor
        def _(pe):
            norm.pe(pe)
            normed = lambda k: pe.wait_ge(norm.out_done, k + 1)
            for p in range(4):
                def free(f):
                    if p < 2:
                        normed(4 * p + f)
                    else:
                        pe.wait_ge(q_out, 4 * (p - 2) + f + 1)
                stream.pe(pe, p, 4 * (p % 2), free, (m.nh, m.nl), False, lambda kt: p or normed(kt))
            pe.wait_ge(keys_in, 16)
            pe.wait_ge(q_out, NHZ)
            for g in range(4 * TT):
                if g >= 8:
                    pe.wait_ge(s_out, g - 7)
                for a in range(4):
                    hz = 4 * (g % 4) + a
                    last = pe.matmul(m.ps[:, g % 8, a * P:(a + 1) * P], qT[:, hz, (g // 4) * P:(g // 4 + 1) * P], keys[:, hz, :],
                                     start=True, stop=True)
                last.then_inc(scored, 1)

        @block.scalar
        def _(act):
            norm.act(act, between=lambda: (stream.high(act, 0), stream.high(act, 1)))

            def copies(p):
                for f in range(4):
                    g = 4 * p + f
                    act.wait_ge(stream.prod, g + 1)
                    act.activation(qT[:, g, :], m.ps[:, g % 8, :], ACT.Copy).then_inc(q_out, 1)

            for p in range(4):
                stream.act(act, p, lambda: copies(p))

        @block.vector
        def _(dve):
            norm.dve(dve)
            for g in range(4 * TT):
                dve.wait_ge(scored, g + 1)
                dve.tensor_copy(m.scores[:, g // 4, 4 * (g % 4):4 * (g % 4) + 4, :].rearrange("p a k -> p (a k)"),
                                m.ps[:, g % 8, :]).then_inc(s_out, 1)


def up_stage(nc, m, g_dense, a_dense, down):
    STEP = 16
    FOURS = STEP // 4
    WITH = P // STEP
    ALONE = 16
    NJ = ALONE + WITH
    PIECES = 8
    TAIL = PEER_K - TT * NJ
    r = m.region(AT_SCORES + 32, AT_END - KB_GATES)
    take = lambda name, shape, dt=F32: r.take(f"up_{name}", shape, dt)
    u, uh, ul = take("u", [P, 2, KT, P]), take("u_high", [P, 2, KT, P], F32R), take("u_low", [P, 2, KT, P], F32R)
    av = take("gelu", [P, 2, T])
    spare = take("spare", [P, NHZ * PEER_K])
    top_v, top_i, top_f = take("top_v", [P, NHZ, TOPK]), take("top_i", [P, NHZ, TOPK], U32), take("top_f", [P, NHZ, TOPK])
    best, pos, part = take("best", [P, PEER_H, TOPK]), take("pos", [P, PEER_H, TOPK], U32), take("part", [P, HK], U32)
    part_f, sums = take("part_f", [P, HK]), take("sums", [P, PEER_H])
    chosen = take("chosen", [P, 3, HK])
    high_t = take("chosen_t", [P, 3, P])
    gate_h, gate_l = take("gate_high", [P, P], F32R), take("gate_low", [P, P])
    hot_i, hot_h, hot_l = (take(f"hot_{x}", [P, STEP, P], F32R) for x in ("first", "high", "low"))
    r = m.region(AT_END - KB_GATES, AT_END)
    gs = take("gates", [P, PEER_K, P])
    sem = lambda name: m.sem(f"up_{name}")
    dve_s, exped, made, turned, t_copied, second_eq, second_low, second_high, spread, gs_done, maxed = (
        sem(x) for x in ("dve_steps", "gate_exp", "gates_made", "turned", "turned_copied", "second_key_found", "gates_low_placed",
                         "gates_high_placed", "spread", "gates_copied", "best_less_max"))
    stored = sem("gates_stored")
    u_in, a_stored = [sem(f"u{n}_loaded") for n in range(2)], [sem(f"gelu{n}_stored") for n in range(2)]
    high, low, prod, gelu = sem("u_high_done"), sem("u_low_done"), sem("products"), sem("gelu_done")
    eu = m.ins["expert_u"]
    with nc.Block() as block:

        @block.sync
        def _(sp):
            for n in range(2):
                sp.sem_inc(a_stored[n], 16)
                sp.dma_start(u[:, n, :, :].rearrange("p k i -> p (k i)"), eu[n]).then_inc(u_in[n], 16)

            def key(j, n, load=True):
                if load:
                    sp.wait_ge(low, j + 1)
                    sp.dma_start(u[:, n, :, :].rearrange("p k i -> p (k i)"),
                                 eu[bass.ds(j + 2, 1)].rearrange("a p k -> p (a k)")).then_inc(u_in[n], 16)
                sp.wait_ge(gelu, j + 3)
                sp.dma_start(a_dense[bass.ds(j, 1)].rearrange("a i t -> i (a t)"), av[:, n, :]).then_inc(a_stored[n], 16)

            def gates_piece(tt, n):
                j = slice(n * (PEER_K // PIECES), (n + 1) * (PEER_K // PIECES))
                sp.dma_start(g_dense[j, :, tt * P:(tt + 1) * P].rearrange("j i t -> i j t"), gs[:, j, :]).then_inc(stored, 16)

            for tt in range(TT):
                if tt:
                    sp.wait_ge(gs_done, tt * (P // 4) + FOURS)
                    for n in range(PIECES):
                        key(tt * NJ + n, n % 2)
                        gates_piece(tt - 1, n)
                with sp.Fori(PIECES // 2 if tt else 0, NJ // 2) as i:
                    for n in range(2):
                        key(i * 2 + (tt * NJ + n), n)
            for n in range(TAIL):
                if n == 0:
                    sp.wait_ge(gs_done, TT * (P // 4) + FOURS)
                j = PEER_K - TAIL + n
                key(j, j % 2, j < PEER_K - 2)
                if n < PIECES:
                    gates_piece(TT - 1, n)
                if n == PIECES + 2:
                    sp.wait_ge(stored, 16 * PIECES * TT)
                    for b in range(2):
                        sp.wait_ge(a_stored[b], 16 * (DOWN_J + 1))
                for b in range(2):
                    first = PIECES + 3 + b * DOWN_J
                    if n in range(first, first + DOWN_J):
                        down.load_v(sp, b, b, n - first)
                    first += 2 * DOWN_J
                    if n in range(first, first + DOWN_J):
                        down.load_weights(sp, b, b, n - first)
            for n in range(2):
                sp.wait_ge(a_stored[n], 16 * (PEER_K // 2 + 1))

        @block.gpsimd
        def _(pool):
            def low_part(j, n):
                pool.wait_ge(high, j + 1)
                pool.tensor_tensor(ul[:, n, :, :], u[:, n, :, :], bits32(uh[:, n, :, :]), ALU.subtract).then_inc(low, 1)

            for n in range(2):
                low_part(n, n)
            for tt in range(TT):
                with pool.Fori(0, ALONE // 2) as i:
                    for n in range(2):
                        low_part(i * 2 + (tt * NJ + n + 2), n)
                with pool.Fori(0, WITH // 2) as i:
                    for n in range(2):
                        for b in range(FOURS):
                            hold(pool, m, second_low, i * (2 * FOURS) + (tt * (P // 4) + n * FOURS + b + 1))
                            t = bass.ds(i * (2 * STEP) + (n * STEP + 4 * b), 4)
                            o = hot_h[:, 4 * b:4 * b + 4, :]
                            pool.tensor_tensor(o, bits32(o), bits32(gate_h[:, t]).unsqueeze(2).broadcast_to([P, 4, P]),
                                               ALU.mult).then_inc(second_high, 1)
                        low_part(i * 2 + (tt * NJ + ALONE + n + 2), n)
            with pool.Fori(0, TAIL // 2 - 1) as i:
                for n in range(2):
                    low_part(i * 2 + (PEER_K - TAIL + n + 2), n)

        @block.vector
        def _(dve):
            st = Steps(dve, dve_s)

            def top16(values, rest, v, i):
                st.done(dve.max(v[:, 0:8], values))
                dve.max_index(i[:, 0:8], v[:, 0:8], values)
                st.done(dve.match_replace(rest, v[:, 0:8], values, NEG))
                st.done(dve.max(v[:, 8:16], rest))
                return dve.max_index(i[:, 8:16], v[:, 8:16], rest)

            flat = lambda x: x.rearrange("p h k -> p (h k)")
            grid = lambda x: x.rearrange("p (h k a) -> p h k a", h=PEER_H, k=TOPK)
            iota = sq(m, "iota")
            iotas = iota.unsqueeze(1).broadcast_to([P, 4, P])
            for tt in range(TT):
                scores = m.scores[:, tt, :, :]
                cand = flat(scores)
                for hz in range(NHZ):
                    last = top16(scores[:, hz, :], spare[:, hz * PEER_K:(hz + 1) * PEER_K], top_v[:, hz, :], top_i[:, hz, :])
                st.done(last)
                dve.tensor_copy(top_f[:, :, :], top_i[:, :, :])
                tv = top_v[:, :, :].rearrange("p (h z) k -> p h z k", z=2)
                st.done(dve.tensor_tensor(grid(cand), tv[:, :, 0, :].unsqueeze(3).broadcast_to([P, PEER_H, TOPK, TOPK]),
                                          tv[:, :, 1, :].unsqueeze(2).broadcast_to([P, PEER_H, TOPK, TOPK]), ALU.add))
                for h in range(PEER_H):
                    c, rest = (x[:, h * TOPK * TOPK:(h + 1) * TOPK * TOPK] for x in (cand, spare))
                    last = top16(c, rest, best[:, h, :], pos[:, h, :])
                st.done(last)
                top1 = best[:, :, 0:1].broadcast_to([P, PEER_H, TOPK])
                gate = chosen[:, 2, :].rearrange("p (h k) -> p h k", k=TOPK)
                dve.tensor_tensor(gate, best[:, :, :], top1, ALU.subtract).then_inc(maxed, 1)
                for z in range(2):
                    if z == 0:
                        st.done(dve.tensor_scalar(part[:, :], flat(pos[:, :, :]), 4, None, ALU.logical_shift_right))
                    else:
                        st.done(dve.tensor_scalar(part[:, :], flat(pos[:, :, :]), 15, None, ALU.bitwise_and))
                    st.done(dve.tensor_copy(part_f[:, :], part[:, :]))
                    eq = spare[:, :].rearrange("p (n a) -> p n a", a=TOPK)
                    st.done(dve.tensor_tensor(eq, part_f[:, :].unsqueeze(2).broadcast_to([P, HK, TOPK]),
                                              iota[:, 0:TOPK].unsqueeze(1).broadcast_to([P, HK, TOPK]), ALU.is_equal))
                    tf = top_f[:, :, :].rearrange("p (h z) k -> p h z k", z=2)[:, :, z, :].unsqueeze(2)
                    st.done(dve.tensor_tensor(grid(spare[:, :]), grid(spare[:, :]), tf.broadcast_to([P, PEER_H, TOPK, TOPK]), ALU.mult))
                    st.done(dve.tensor_reduce(chosen[:, z, :], eq, AX.X, ALU.add))
                dve.wait_ge(exped, tt + 1)
                st.done(dve.tensor_reduce(sums[:, :], gate, AX.X, ALU.add))
                st.done(dve.reciprocal(sums[:, :], sums[:, :]))
                dve.tensor_tensor(gate, gate, sums[:, :].unsqueeze(2).broadcast_to([P, PEER_H, TOPK]), ALU.mult).then_inc(made, 1)
                dve.wait_ge(t_copied, tt + 1)
                st.done(dve.tensor_tensor(gate_l[:, :], high_t[:, 2, :], bits32(gate_h[:, :]), ALU.subtract))
                with dve.Fori(0, WITH) as i:
                    for b in range(FOURS):
                        k = i * FOURS + (tt * (P // 4) + b + 1)
                        four, t = slice(4 * b, 4 * b + 4), bass.ds(i * STEP + 4 * b, 4)
                        spread_over = lambda x: x.unsqueeze(2).broadcast_to([P, 4, P])
                        dve.wait_ge(spread, k)
                        dve.tensor_tensor(hot_h[:, four, :], iotas, spread_over(high_t[:, 1, t]), ALU.is_equal).then_inc(second_eq, 1)
                        dve.tensor_tensor(hot_i[:, four, :], iotas, spread_over(high_t[:, 0, t]), ALU.is_equal)
                        dve.wait_ge(second_eq, k)
                        dve.tensor_tensor(hot_l[:, four, :], bits32(hot_h[:, four, :]), spread_over(gate_l[:, t]), ALU.mult).then_inc(second_low, 1)

        @block.scalar
        def _(act):
            act.sem_inc(gs_done, FOURS)
            act.sem_inc(gelu, 2)

            def split(j, n):
                act.wait_ge(u_in[n], j * 8 + (16 - 8 * n))
                act.activation(uh[:, n, :, :], u[:, n, :, :], ACT.Copy).then_inc(high, 1)

            def key(j, n, more=True):
                act.wait_ge(prod, j + 1)
                act.wait_ge(a_stored[n], j * 8 + (16 - 8 * n))
                act.activation(av[:, n, :], m.ps[:, n, :], ACT.Gelu).then_inc(gelu, 1)
                if more:
                    split(j + 2, n)

            for n in range(2):
                split(n, n)
            for tt in range(TT):
                gate = chosen[:, 2, :]
                with act.Fori(0, ALONE // 2) as i:
                    for n in range(2):
                        key(i * 2 + (tt * NJ + n), n)
                act.wait_ge(maxed, tt + 1)
                act.activation(gate, gate, ACT.Exp).then_inc(exped, 1)
                act.wait_ge(turned, tt + 1)
                act.activation(high_t[:, :, :], m.ps[:, 6, 0:3 * P].rearrange("p (a n) -> p a n", a=3), ACT.Copy)
                act.activation(gate_h[:, :], m.ps[:, 6, 2 * P:3 * P], ACT.Copy).then_inc(t_copied, 1)

                if tt:
                    act.wait_ge(stored, 16 * PIECES * tt)
                with act.Fori(0, WITH // 2) as i:
                    for n in range(2):
                        key(i * 2 + (tt * NJ + ALONE + n), n)
                        for b in range(FOURS):
                            k = tt * (P // 4) + n * FOURS + b
                            hold(act, m, spread, i * (2 * FOURS) + (k + 1 + FOURS))
                            dst = gs[:, :, bass.ds(i * (2 * STEP) + (n * STEP + 4 * b), 4)].rearrange("p j t -> p t j")
                            act.activation(dst, m.ps[:, 2 + b, :].rearrange("p (t j) -> p t j", t=4), ACT.Copy).then_inc(gs_done, 1)
            with act.Fori(0, TAIL // 2 - 1) as i:
                for n in range(2):
                    key(i * 2 + (PEER_K - TAIL + n), n)
            for n in range(2):
                key(PEER_K - 2 + n, n, False)

        @block.tensor
        def _(pe):
            pe.sem_inc(spread, FOURS)

            def key(j, n):
                pe.wait_ge(low, j + 1)
                pe.wait_ge(gelu, j + 1)
                products(pe, m.ps[:, n, :], [(uh[:, n, k, :], ul[:, n, k, :]) for k in range(KT)],
                         [(m.nh[:, k, :], m.nl[:, k, :]) for k in range(KT)]).then_inc(prod, 1)

            for tt in range(TT):
                with pe.Fori(0, ALONE // 2) as i:
                    for n in range(2):
                        key(i * 2 + (tt * NJ + n), n)
                pe.wait_ge(made, tt + 1)
                for n in range(3):
                    last = pe.transpose(m.ps[:, 6, n * P:(n + 1) * P], chosen[:, n, :], sq(m, "eye"))
                last.then_inc(turned, 1)
                with pe.Fori(0, WITH // 2) as i:
                    for n in range(2):
                        key(i * 2 + (tt * NJ + ALONE + n), n)
                        for b in range(FOURS):
                            k = tt * (P // 4) + n * FOURS + b
                            pe.wait_ge(second_low, i * (2 * FOURS) + (k + 1))
                            pe.wait_ge(second_high, i * (2 * FOURS) + (k + 1))
                            pe.wait_ge(gs_done, i * (2 * FOURS) + (k + 1))
                            for q in range(4 * b, 4 * b + 4):
                                o = m.ps[:, 2 + b, (q % 4) * P:(q % 4 + 1) * P]
                                pe.matmul(o, hot_i[:, q, :], hot_h[:, q, :], start=True, stop=False)
                                last = pe.matmul(o, hot_i[:, q, :], hot_l[:, q, :], start=False, stop=True)
                            last.then_inc(spread, 1)
            with pe.Fori(0, TAIL // 2) as i:
                for n in range(2):
                    key(i * 2 + (PEER_K - TAIL + n), n)


class DownLoads:

    def __init__(self, nc, m, g_dense, a_dense):
        r = m.region(AT_END - KB_GATES, AT_END)
        self.v = r.take("down_v", [P, 2, DOWN_J, D])
        self.a, self.g = (r.take(f"down_{x}", [P, 2, DOWN_J, T]) for x in ("gelu", "gates"))
        self.v_in, self.a_in, self.g_in = ([nc.alloc_semaphore(name=f"down_{x}{b}_loaded") for b in range(2)] for x in "vag")
        self.ev = m.ins["expert_v"].rearrange("p (j n) -> p j n", n=D)
        self.ad, self.gd = (x.rearrange("j i t -> i j t") for x in (a_dense, g_dense))

    def load_v(self, sp, n, b, j):
        sp.dma_start(self.v[:, b, j:j + 1, :], self.ev[:, bass.ds(n * DOWN_J + j, 1), :]).then_inc(self.v_in[b], 16)

    def load_weights(self, sp, n, b, j):
        sp.dma_start(self.a[:, b, j:j + 1, :], self.ad[:, bass.ds(n * DOWN_J + j, 1), :]).then_inc(self.a_in[b], 16)
        sp.dma_start(self.g[:, b, j:j + 1, :], self.gd[:, bass.ds(n * DOWN_J + j, 1), :]).then_inc(self.g_in[b], 16)


def down_stage(nc, m, down):
    JB = DOWN_J
    NB = PEER_K // JB
    r = m.region(AT_XT, AT_END - KB_GATES)
    take = lambda name, shape, dt=F32: r.take(f"down_{name}", shape, dt)
    v, a, g, v_in, a_in, g_in = down.v, down.a, down.g, down.v_in, down.a_in, down.g_in
    vh, vl = ([take(f"v{b}_{x}", [P, JB, D], F32R) for b in range(2)] for x in ("high", "low"))
    wh, wl = take("w_high", [P, 2, JB, T], F32R), take("w_low", [P, 2, JB, T], F32R)
    m.sems += v_in + a_in + g_in
    sem = lambda name: m.sem(f"down_{name}")
    prod, weighed, w_high, w_low, v_high, v_low, added = (sem(x) for x in ("products", "weighed", "w_high_done", "w_low_done",
                                                                           "v_high_done", "v_low_done", "added"))
    with nc.Block() as block:

        @block.sync
        def _(sp):
            with sp.Fori(1, NB // 2) as i:
                for b in range(2):
                    sp.wait_ge(w_low, i * (2 * JB) + (b - 1) * JB)
                    for j in range(JB):
                        down.load_weights(sp, i * 2 + b, b, j)
                    sp.wait_ge(v_low, i * (2 * JB) + (b - 1) * JB)
                    for j in range(JB):
                        down.load_v(sp, i * 2 + b, b, j)

        @block.scalar
        def _(act):
            with act.Fori(0, NB // 2) as i:
                for b in range(2):
                    act.wait_ge(v_in[b], i * (16 * JB) + 16 * JB)
                    act.wait_ge(prod, i * 16 + (8 * b + 8))
                    for j in range(JB):
                        act.activation(vh[b][:, j, :], v[:, b, j, :], ACT.Copy).then_inc(v_high, 1)
                        act.wait_ge(weighed, i * (2 * JB) + (b * JB + j + 1))
                        act.activation(wh[:, b, j, :], a[:, b, j, :], ACT.Copy).then_inc(w_high, 1)

        @block.gpsimd
        def _(pool):
            with pool.Fori(0, NB // 2) as i:
                for b in range(2):
                    for j in range(JB):
                        pool.wait_ge(v_high, i * (2 * JB) + (b * JB + j + 1))
                        pool.tensor_tensor(vl[b][:, j, :], v[:, b, j, :], bits32(vh[b][:, j, :]), ALU.subtract).then_inc(v_low, 1)

        @block.vector
        def _(dve):
            def weigh(n, b, row_by_row=False):
                use = (n * 8 + (16 - 8 * b)) * JB
                dve.wait_ge(a_in[b], use)
                dve.wait_ge(g_in[b], use)

                def low(j):
                    dve.wait_ge(w_high, n * JB + (j + 1))
                    dve.tensor_tensor(wl[:, b, j, :], a[:, b, j, :], bits32(wh[:, b, j, :]), ALU.subtract).then_inc(w_low, 1)

                for j in range(JB):
                    dve.tensor_tensor(a[:, b, j, :], a[:, b, j, :], g[:, b, j, :], ALU.mult).then_inc(weighed, 1)
                    if row_by_row and j:
                        low(j - 1)
                for j in range(JB - 1 if row_by_row else 0, JB):
                    low(j)

            def add(n):
                for q in range(8):
                    half, tt = divmod(q, 4)
                    dve.wait_ge(prod, n * 8 + (16 + q + 1))
                    o = m.h[:, tt, half * CW:(half + 1) * CW]
                    dve.tensor_tensor(o, o, m.ps[:, q, :], ALU.add).then_inc(added, 1)

            dve.sem_inc(added, 8)
            weigh(0, 0, True)
            with dve.Fori(0, NB // 2 - 1) as i:
                weigh(i * 2 + 1, 1)
                add(i * 2)
                weigh(i * 2 + 2, 0)
                add(i * 2 + 1)
            weigh(NB - 1, 1)
            add(NB - 2)
            add(NB - 1)

        @block.tensor
        def _(pe):
            pe.sem_inc(prod, 16)

            def tile(q):
                half, tt = divmod(q, 4)
                return slice(tt * P, (tt + 1) * P), slice(half * CW, (half + 1) * CW)

            def block_products(i, b):
                pe.wait_ge(v_low, i * (2 * JB) + (b + 1) * JB)
                pe.wait_ge(w_low, i * (2 * JB) + (b + 1) * JB)
                for q in range(8):
                    t, c = tile(q)
                    pe.wait_ge(added, i * 16 + (8 * b + q + 1))
                    products(pe, m.ps[:, q, :], [(wh[:, b, j, t], wl[:, b, j, t]) for j in range(JB)],
                             [(vh[b][:, j, c], vl[b][:, j, c]) for j in range(JB)]).then_inc(prod, 1)

            pe.wait_ge(added, 8)
            for j in range(JB):
                pe.wait_ge(v_low, j + 1)
                pe.wait_ge(w_low, j + 1)
                for q in range(8):
                    t, c = tile(q)
                    for n, (x, y) in enumerate(((wh, vh), (wh, vl), (wl, vh))):
                        last = pe.matmul(m.ps[:, q, :], x[:, 0, j, t], y[0][:, j, c], start=j + n == 0, stop=j == JB - 1 and n == 2)
                    if j == JB - 1:
                        last.then_inc(prod, 1)
            block_products(0, 1)
            with pe.Fori(1, NB // 2) as i:
                for b in range(2):
                    block_products(i, b)


def output_stage(nc, m):
    KP = PLE // P
    r = m.region(AT_XT, AT_END)
    norm = NormT(nc, m, r, "ple_norm", COL_PLE)
    pT = r.take("p_t", [P, KP, T])
    wp = r.take("w_ple_proj", [P, 2, KP, CW])
    gain = r.take("final_gain", [P, D])
    sg = r.take("ple_gate", [P, 4, CW])
    fin = r.take("final_stat", [P, 3, TT])
    y = norm.xs
    (g_out, gate, added, squared, meaned, rooted, dve_s, y_done, p_in, stored) = (
        m.sem(f"ple_{x}") for x in ("projected", "gate", "added", "squared", "meaned", "rooted", "dve_steps",
                                    "y_done", "p_loaded", "stored"))
    stream = Stream(m, r, r, "ple", [m.ins["w_ple_gate"][n] for n in range(2)])
    with nc.Block() as block:

        @block.sync
        def _(sp):
            sp.dma_start(pT[:, :, :], m.ins["p_t"].rearrange("p (k t) -> p k t", t=T)).then_inc(p_in, 16)
            sp.dma_start(wp[:, :, :, :].rearrange("p n k c -> p n (k c)"), m.ins["w_ple_proj"].rearrange("n p c -> p n c")).then_inc(p_in, 16)
            sp.dma_start(gain[:, :], m.ins["norm_final"].broadcast_to([P, D])).then_inc(p_in, 16)
            stream.sp(sp)
            for tt in range(TT):
                sp.wait_ge(y_done, tt + 1)
                sp.dma_start(m.outs[tt // TS][0, (tt % TS) * P:(tt % TS + 1) * P, :], y[:, tt, :]).then_inc(stored, 16)
            sp.wait_ge(stored, 16 * TT)

        @block.gpsimd
        def _(pool):
            stream.pool(pool)

        @block.tensor
        def _(pe):
            norm.pe(pe)
            normed = lambda k: pe.wait_ge(norm.out_done, k + 1)
            for n in range(2):
                if n == 0:
                    stream.pe(pe, n, 0, normed, (m.nh, m.nl), True, normed)
                    pe.wait_ge(p_in, 48)
                for tt in range(TT):
                    if n:
                        pe.wait_ge(added, tt + 1)
                    for k in range(KP):
                        last = pe.matmul(m.ps[:, 4 + tt, :], pT[:, k, tt * P:(tt + 1) * P], wp[:, n, k, :], start=k == 0, stop=k == KP - 1)
                    last.then_inc(g_out, 1)
                if n:
                    stream.pe(pe, n, 0, lambda tt: pe.wait_ge(gate, tt + 1), (m.nh, m.nl), True)

        @block.scalar
        def _(act):
            norm.act(act, between=lambda: (stream.high(act, 0), stream.high(act, 1)))

            def gates(n):
                for tt in range(TT):
                    g = 4 * n + tt
                    act.wait_ge(stream.prod, g + 1)
                    if g >= 4:
                        act.wait_ge(added, g - 3)
                    act.activation(sg[:, g % 4, :], m.ps[:, g % 4, :], ACT.Sigmoid).then_inc(gate, 1)

            for n in range(2):
                stream.act(act, n, lambda: gates(n))
            for tt in range(TT):
                act.wait_ge(added, 4 + tt + 1)
                act.activation(y[:, tt, :], m.h[:, tt, :], ACT.Square, accum_out=fin[:, 0, tt:tt + 1]).then_inc(squared, 1)
            act.wait_ge(meaned, 1)
            act.activation(fin[:, 2, :], fin[:, 1, :], ACT.Sqrt).then_inc(rooted, 1)

        @block.vector
        def _(dve):
            norm.dve(dve)
            st = Steps(dve, dve_s)
            for g in range(8):
                n, tt = divmod(g, 4)
                dve.wait_ge(gate, g + 1)
                dve.wait_ge(g_out, g + 1)
                st.done(dve.tensor_tensor(sg[:, tt, :], m.ps[:, 4 + tt, :], sg[:, tt, :], ALU.mult))
                o = m.h[:, tt, n * CW:(n + 1) * CW]
                dve.tensor_tensor(o, o, sg[:, tt, :], ALU.add).then_inc(added, 1)
            dve.wait_ge(squared, TT)
            dve.tensor_scalar(fin[:, 1, :], fin[:, 0, :], 1.0 / D, EPS, ALU.mult, ALU.add).then_inc(meaned, 1)
            dve.wait_ge(rooted, 1)
            dve.wait_ge(p_in, 48)
            st.done(dve.reciprocal(fin[:, 0, :], fin[:, 2, :]))
            for tt in range(TT):
                dve.scalar_tensor_tensor(y[:, tt, :], m.h[:, tt, :], fin[:, 0, tt:tt + 1], gain[:, :],
                                         ALU.mult, ALU.mult).then_inc(y_done, 1)


def layouts(**a):
    f = {k: np.asarray(v) for k, v in a.items()}
    chunk = lambda w: np.ascontiguousarray(w.reshape(w.shape[0] // P, P, w.shape[1] // CW, CW).transpose(2, 1, 0, 3)
                                           .reshape(w.shape[1] // CW, P, -1))
    cols = lambda v: v.reshape(-1, P).T
    w = f["w_in"][0]
    at = np.cumsum([0, 1024, 2048, 32, 3072, 1024, 16, 16, 1024, 1024])
    part = lambda n: w[:, at[n]:at[n + 1]]
    conv_w = np.concatenate([part(1), part(3)], axis=1)
    gates = np.concatenate([part(0), part(7), part(4), part(8)], axis=1)
    small = np.concatenate([part(2), part(5), part(6)], axis=1)
    taps = np.concatenate([f["ssd_conv_w"][0], f["gdn_conv_w"][0]], axis=1)
    bias = np.concatenate([f["ssd_conv_b"][0], np.zeros(3 * GDN_H * GDN_D, np.float32)])
    conv = np.concatenate([taps, bias[None]], axis=0).reshape(5, N_CONV, P).transpose(2, 1, 0).reshape(P, -1)
    colp = np.concatenate([conv, cols(f["norm_mix"][0]), cols(f["norm_ffn"][0]), cols(f["norm_ple"][0]),
                           cols(f["ssd_norm"][0]), cols(f["gdn_norm"][0])], axis=1)
    rowp = np.concatenate([f["ssd_dt_bias"][0].ravel(), f["gdn_dt_bias"][0].ravel(), f["ssd_a_log"][0].ravel(),
                           f["gdn_a_log"][0].ravel(), f["ssd_d"][0]])[None]
    eu = f["expert_u"][0].reshape(P, PEER_K, KT, P)
    ev = f["expert_v"][0].reshape(P, PEER_K * D)
    keys = f["peer_keys"][0].reshape(NHZ, PEER_K, P).transpose(2, 0, 1).reshape(P, NHZ * PEER_K)
    d = {
        "x_prompt": f["x_prompt"], "x_sample": f["x_sample"],
        "p_t": np.concatenate([f["p_prompt"][0, 0], f["p_sample"][0, 0]], axis=0).T.reshape(PLE // P, P, T).transpose(1, 0, 2)
        .reshape(P, -1),
        "squares": squares(), "halves": halves(), "norm_final": f["norm_final"][None], "column_params": colp, "row_params": rowp,
        "w_conv": np.ascontiguousarray(conv_w.reshape(KT, P, -1, 2 * P).transpose(2, 1, 0, 3)).reshape(-1, P, KT * 2 * P),
        "w_gates": chunk(gates),
        "w_small": small.reshape(KT, P, 64).transpose(1, 0, 2).reshape(P, -1),
        "w_ssd_out": chunk(f["w_ssd_out"][0]), "w_gdn_out": chunk(f["w_gdn_out"][0]), "w_out": chunk(f["w_out"][0]),
        "peer_query": chunk(f["peer_query"][0]), "w_ple_gate": chunk(f["w_ple_gate"][0]),
        "w_ple_proj": chunk(f["w_ple_proj"][0]),
        "peer_keys": keys,
        "expert_u": eu.transpose(1, 3, 2, 0).reshape(PEER_K, P, D),
        "expert_v": ev,
    }
    return {k: np.ascontiguousarray(v) for k, v in d.items()}


def program(nc, arrays):
    ins = {k: nc.dram_tensor(k, a.shape, F32, kind="ExternalInput").ap() for k, a in arrays.items()}
    outs = [nc.dram_tensor(n, (1, L, D), F32, kind="ExternalOutput").ap() for n in ("y_prompt", "y_sample")]
    build(nc, ins, outs)


def kernel(**inputs):
    import concourse.bacc as bacc
    from concourse.bass_utils import run_bass_kernel_spmd

    arrays = layouts(**inputs)
    nc = bacc.Bacc("TRN2", target_bir_lowering=False, num_devices=1, dynamic_dma_scratch_size=1024)
    program(nc, arrays)
    r = run_bass_kernel_spmd(nc, [arrays], core_ids=[0])
    return r.results[0]["y_prompt"], r.results[0]["y_sample"]
```
